# Optimizing a Trainium2 kernel written in Bass

```python
import jax, jax.numpy as jnp
from jax import lax
import numpy as np

D_MODEL = 2048
BATCH = 1
SEQ = 256
DEPTH = 1

N_META = 16
EPS = 1e-6
HG_HEADS = 8
HG_KDIM = 128
HG_VDIM = 128
HG_WIDTH_K = HG_HEADS * HG_KDIM
HG_WIDTH_V = HG_HEADS * HG_VDIM
HG_CHUNK = 64
AT_HEADS = 8
AT_HDIM = 128
AT_WIDTH = AT_HEADS * AT_HDIM
IDX_HEADS = 16
IDX_HDIM = 64
IDX_TOPK_MAX = 256
Q_BLOCK = 128
D_FF = 5632
CONV_W = 3
IN_SIZES = (HG_WIDTH_K, HG_WIDTH_K, HG_WIDTH_V, HG_WIDTH_V,
            AT_WIDTH, AT_WIDTH, AT_WIDTH,
            IDX_HEADS * IDX_HDIM, IDX_HDIM, IDX_HEADS,
            D_MODEL, D_MODEL)
D_IN = sum(IN_SIZES)

kernel_name = "hgrn2_dsa_gated_hybrid_block"

def rmsnorm(x, w):
    xf = x.astype(jnp.float32)
    y = xf * lax.rsqrt(jnp.mean(xf * xf, axis=-1, keepdims=True) + EPS)
    return (y * w.astype(jnp.float32)).astype(x.dtype)

def split_cols(z, sizes):
    offs = []
    acc = 0
    for s in sizes[:-1]:
        acc += s
        offs.append(acc)
    return jnp.split(z, offs, axis=-1)

def hgrn2_mix(q_raw, f_raw, i_raw, g_raw, lb, norm_w):
    B, T, _ = q_raw.shape
    f32 = jnp.float32
    H, dk, dv, C = HG_HEADS, HG_KDIM, HG_VDIM, HG_CHUNK
    q = jax.nn.silu(q_raw.astype(f32))
    z = f_raw.astype(f32)
    lbf = lb.astype(f32)
    lf = jnp.log(lbf + (1.0 - lbf) * jax.nn.sigmoid(z))
    kc = (1.0 - lbf) * jax.nn.sigmoid(-z)
    v = i_raw.astype(f32)
    pad = (-N_META) % C
    Tp = T + pad
    N = Tp // C

    def to_chunks(a, d):
        a = jnp.pad(a, ((0, 0), (pad, 0), (0, 0)))
        return a.reshape(B, N, C, H, d).transpose(1, 0, 3, 2, 4)

    mask = jnp.tril(jnp.ones((C, C), dtype=bool))

    def step(S, inp):
        qc, kcc, vc, lfc = inp
        b = jnp.cumsum(lfc, axis=2)
        o_inter = jnp.einsum('bhtd,bhde->bhte', qc * jnp.exp(b), S)
        diff = b[:, :, :, None, :] - b[:, :, None, :, :]
        decay = jnp.exp(jnp.where(mask[None, None, :, :, None], diff, -jnp.inf))
        A = jnp.einsum('bhtd,bhtsd,bhsd->bhts', qc, decay, kcc)
        o = o_inter + jnp.einsum('bhts,bhse->bhte', A, vc)
        b_last = b[:, :, -1:, :]
        S = jnp.exp(b_last[:, :, 0, :])[..., None] * S + jnp.einsum(
            'bhsd,bhse->bhde', kcc * jnp.exp(b_last - b), vc)
        return S, o

    S0 = jnp.zeros((B, H, dk, dv), f32)
    _, o = lax.scan(step, S0, (to_chunks(q, dk), to_chunks(kc, dk),
                               to_chunks(v, dv), to_chunks(lf, dk)))
    o = o.transpose(1, 0, 3, 2, 4).reshape(B, Tp, H, dv)[:, pad:]
    o = rmsnorm(o, norm_w) * jax.nn.silu(g_raw.astype(f32).reshape(B, T, H, dv))
    return o.reshape(B, T, H * dv).astype(q_raw.dtype)

def causal_dwconv(u, w, b):
    Cn = u.shape[-1]
    y = lax.conv_general_dilated(u, w[:, None, :].astype(u.dtype), window_strides=(1,),
                                 padding=[(CONV_W - 1, 0)],
                                 dimension_numbers=('NWC', 'WIO', 'NWC'),
                                 feature_group_count=Cn)
    return y + b.astype(u.dtype)

def dsa_mix(q, k, v, qi, ki, wi, topk):
    B, T, _ = q.shape
    f32 = jnp.float32
    q = q.reshape(B, T, AT_HEADS, AT_HDIM)
    k = k.reshape(B, T, AT_HEADS, AT_HDIM)
    v = v.reshape(B, T, AT_HEADS, AT_HDIM)
    qi = qi.reshape(B, T, IDX_HEADS, IDX_HDIM)
    wi = wi * (IDX_HEADS ** -0.5)
    nb = -(-T // Q_BLOCK)
    Tq = nb * Q_BLOCK

    def blocks(a):
        a = jnp.pad(a, [(0, 0), (0, Tq - T)] + [(0, 0)] * (a.ndim - 2))
        return a.reshape((B, nb, Q_BLOCK) + a.shape[2:]).swapaxes(0, 1)

    key_pos = jnp.arange(T)
    gather = jax.vmap(lambda a, i: a[i])

    def block(inp):
        bi, qb, qib, wib = inp
        qpos = bi * Q_BLOCK + jnp.arange(Q_BLOCK)
        causal = key_pos[None, :] <= qpos[:, None]
        s_idx = jnp.einsum('bqhd,bsd->bqhs', qib, ki) * (IDX_HDIM ** -0.5)
        score = jnp.einsum('bqh,bqhs->bqs', wib, jax.nn.relu(s_idx)).astype(f32)
        score = jnp.where(causal[None], score, -jnp.inf)
        _, sel = lax.top_k(score, topk)
        valid = sel <= qpos[None, :, None]
        k_sel = gather(k, sel)
        v_sel = gather(v, sel)
        logits = jnp.einsum('bqhd,bqkhd->bqhk', qb, k_sel).astype(f32) * (AT_HDIM ** -0.5)
        logits = jnp.where(valid[:, :, None, :], logits, -jnp.inf)
        p = jax.nn.softmax(logits, axis=-1).astype(v.dtype)
        return jnp.einsum('bqhk,bqkhd->bqhd', p, v_sel)

    out = lax.map(block, (jnp.arange(nb), blocks(q), blocks(qi), blocks(wi)))
    return out.swapaxes(0, 1).reshape(B, Tq, AT_WIDTH)[:, :T]

def setup_inputs(seed: int = 0) -> dict:
    key = jax.random.key(seed)
    ks = jax.random.split(key, 20)
    nrm = jax.random.normal
    f32 = jnp.float32

    def gain(k, shape):
        return 1.0 + 0.02 * nrm(k, shape, f32)

    return {
        "x": nrm(ks[0], (BATCH, SEQ, D_MODEL), f32),
        "meta_tokens": nrm(ks[1], (N_META, D_MODEL), f32),
        "attn_norm_w": gain(ks[2], (DEPTH, D_MODEL)),
        "w_in": nrm(ks[3], (DEPTH, D_MODEL, D_IN), f32) * D_MODEL ** -0.5,
        "hgrn_lb_logits": 0.5 * nrm(ks[4], (DEPTH + 1, HG_WIDTH_K), f32),
        "hgrn_norm_w": gain(ks[5], (DEPTH, HG_VDIM)),
        "idx_k_norm_w": gain(ks[6], (DEPTH, IDX_HDIM)),
        "w_branch_hgrn": nrm(ks[7], (DEPTH, HG_WIDTH_V, D_MODEL), f32) * HG_WIDTH_V ** -0.5,
        "w_branch_dsa": nrm(ks[8], (DEPTH, AT_WIDTH, D_MODEL), f32) * AT_WIDTH ** -0.5,
        "w_out": nrm(ks[9], (DEPTH, D_MODEL, D_MODEL), f32) * D_MODEL ** -0.5,
        "ffn_norm_w": gain(ks[10], (DEPTH, D_MODEL)),
        "w_ffn_gate": nrm(ks[11], (DEPTH, D_MODEL, D_FF), f32) * D_MODEL ** -0.5,
        "w_ffn_up": nrm(ks[12], (DEPTH, D_MODEL, D_FF), f32) * D_MODEL ** -0.5,
        "ffn_conv_w": nrm(ks[13], (DEPTH, CONV_W, D_FF), f32) * CONV_W ** -0.5,
        "ffn_conv_b": 0.01 * nrm(ks[14], (DEPTH, D_FF), f32),
        "w_ffn_down": nrm(ks[15], (DEPTH, D_FF, D_MODEL), f32) * D_FF ** -0.5,
        "final_norm_w": gain(ks[16], (D_MODEL,)),
    }

def reference(x, meta_tokens, attn_norm_w, w_in, hgrn_lb_logits, hgrn_norm_w, idx_k_norm_w,
              w_branch_hgrn, w_branch_dsa, w_out, ffn_norm_w, w_ffn_gate, w_ffn_up,
              ffn_conv_w, ffn_conv_b, w_ffn_down, final_norm_w):
    B, L, _ = x.shape
    topk = min(IDX_TOPK_MAX, L // 4)
    meta = jnp.broadcast_to(meta_tokens.astype(x.dtype)[None], (B, N_META, D_MODEL))
    h = jnp.concatenate([meta, x], axis=1)
    lbs = jnp.cumsum(jax.nn.softmax(hgrn_lb_logits.astype(jnp.float32), axis=0), axis=0)
    for l in range(DEPTH):
        u = rmsnorm(h, attn_norm_w[l])
        z = u @ w_in[l]
        hq, hf, hi, hg, aq, ak, av, iq, ik, iw, ga, gb = split_cols(z, IN_SIZES)
        y_h = hgrn2_mix(hq, hf, hi, hg, lbs[l], hgrn_norm_w[l])
        y_a = dsa_mix(aq, ak, av, iq, rmsnorm(ik, idx_k_norm_w[l]), iw, topk)
        m = (jax.nn.sigmoid(ga) * (y_h @ w_branch_hgrn[l])
             + jax.nn.sigmoid(gb) * (y_a @ w_branch_dsa[l]))
        h = h + m @ w_out[l]
        u = rmsnorm(h, ffn_norm_w[l])
        a = causal_dwconv(u @ w_ffn_gate[l], ffn_conv_w[l], ffn_conv_b[l])
        h = h + (jax.nn.silu(a) * (u @ w_ffn_up[l])) @ w_ffn_down[l]
    return rmsnorm(h, final_norm_w)[:, N_META:]


_drawn_inputs = setup_inputs


def setup_inputs(seed=0):
    import zlib

    import numpy as np

    out = dict(_drawn_inputs(seed))
    spreads = {}
    factors = {'attn_norm_w': 2.87,
     'hgrn_lb_logits': 2.773,
     'hgrn_norm_w': 6.902,
     'idx_k_norm_w': 3.861,
     'ffn_norm_w': 3.937,
     'ffn_conv_b': 28.5,
     'final_norm_w': 8.42}
    for name, (base, spread) in spreads.items():
        noise = np.random.default_rng([zlib.crc32(name.encode()), seed]).standard_normal(out[name].shape)
        drawn = base * np.exp(spread * noise) if base else spread * noise
        out[name] = __import__('jax').numpy.asarray(drawn.astype(out[name].dtype))
    for name, factor in factors.items():
        out[name] = (out[name] * factor).astype(out[name].dtype)
    return out
```

```python
from contextlib import ExitStack

import concourse.bass as bass
from concourse import mybir

F32 = mybir.dt.float32
F32R = mybir.dt.float32r
ACT = mybir.ActivationFunctionType
ALU = mybir.AluOpType
AX = mybir.AxisListType
ds = bass.ds

P = 128
D = 2048
KT = D // P
META, SEQ = 16, 256
T = META + SEQ
T0 = META - 2
TQ = T - T0
HEADS = 8
FF = 5632
FT = FF // P
FH = FT // 2
CH = 16
NC = T // CH
IDXH = 16
TOPK = 64
EPS = 1e-6
SCALE = float(P) ** -0.5
BIG = 2.0 ** 100
FUTURE = -2.0 ** 126
TAKEN = -2.0 ** 127

U_IQ = 0
U_KI = U_IQ + 8
U_QFI = U_KI + 2
U_GATE = U_QFI + 24
U_ATT = U_GATE + 32
U_G = U_ATT + 24
U_MERGE = U_G + 8
U_OUT = U_MERGE + 16
U_FF = U_OUT + 16
U_DOWN = U_FF + 2 * FH
U_FF2 = U_DOWN + FH
U_DOWN2 = U_FF2 + 2 * FH
U_END = U_DOWN2 + FH
C_HQ, C_HG, C_AQ, C_IQ, C_IK, C_IW, C_GA, C_GB = 0, 3072, 4096, 7168, 8192, 8256, 8272, 10320

V_ATTN, V_FFN, V_LB0, V_LB1, V_HGN, V_IDXK, V_CB = 0, 16, 32, 40, 48, 49, 50
V_A = 94
V_C0, V_C1, V_B = 0, 44, 88
V_C2, V_FIN, V_C = 0, 44, 60

UPDATE_BANKS = (3, 4, 6, 7)
ZB = HEADS * T * 4


class Steps:

    def __init__(self, sem):
        self.sem, self.base, self.per, self.i, self.j = sem, 0, 0, None, 0

    def enter(self, i, per):
        self.base, self.i, self.per, self.j = self.base + self.j, i, per, 0

    def leave(self, times):
        assert self.j == self.per, (self.j, self.per)
        self.base, self.i, self.j = self.base + self.per * times, None, 0

    def value(self):
        return self.base + self.j if self.i is None else self.i * self.per + (self.base + self.j)

    def link(self, eng, ins):
        ins.then_inc(self.sem, 1)
        self.j += 1
        eng.wait_ge(self.sem, self.value())


def hybrid_block(nc, x, meta_tokens, attn_norm_w, w_in, hgrn_lb_logits, hgrn_norm_w, idx_k_norm_w,
                 w_branch_hgrn, w_branch_dsa, w_out, ffn_norm_w, w_ffn_gate, w_ffn_up,
                 ffn_conv_w, ffn_conv_b, w_ffn_down, final_norm_w, out):
    ctx = ExitStack()
    with ctx:
        SLAB = 212832
        ctx.enter_context(nc.sbuf_tensor("slab", [P, SLAB // 4], F32))
        ORIGIN = 16512

        def at(name, offset, shape, dt=F32):
            size = 4
            for n in shape[1:]:
                size *= n
            assert offset + size <= SLAB, (name, offset + size)
            return nc.alloc_sbuf_tensor_at(name, shape, dt, offset=ORIGIN + offset, align_bytes=8)

        raw = [at(f"raw{i}", 16384 * i, [P, KT, 256]) for i in range(2)]
        raw_b = [t[:].rearrange("p (b k) c -> p b k c", b=2) for t in raw]
        raw_d = [t[:].rearrange("p (a g) c -> p a (g c)", a=2) for t in raw]
        w_hi = [at(f"w_hi{i}", 32768 + 8192 * i, [P, KT, P], F32R) for i in range(4)]
        w_lo = [at(f"w_lo{i}", 65536 + 8192 * i, [P, KT, P], F32R) for i in range(4)]
        UA = 98304
        u_hi = at("u_hi", UA, [P, KT, T], F32R)
        u_lo = at("u_lo", UA + 17408, [P, KT, T], F32R)
        m_hi = at("m_hi", UA, [P, KT, TQ], F32R)
        m_lo = at("m_lo", UA + 17408, [P, KT, TQ], F32R)
        R = [133120 + ZB * j for j in range(9)]
        BIAS = R[8]
        STG = BIAS + 2304
        CON = STG + 4112

        x_tok = [at(f"x_tok{i}", R[0] + 8192 * i, [P, D]) for i in range(3)]
        junk = at("junk", R[0] + 24576, [P, D])
        vec_rows = at("vec_rows", R[7], [P, 3, P])
        z_qf = at("z_qf", R[0], [P, 2 * HEADS, T])
        z_q, z_k = z_qf[:, 0:HEADS, :], z_qf[:, HEADS:2 * HEADS, :]
        z_v = at("z_v", R[2], [P, HEADS, T])
        band = at("band", R[3], [P, HEADS, T])
        band_rows = at("band_rows", R[6], [CH, HEADS, T])
        z_b = at("z_b", R[4], [P, HEADS, T])
        sig = at("sig", R[5], [P, HEADS, T])
        iq = at("iq", R[6], [P, 8, TQ])
        k_raw = at("k_raw", R[5], [P, T])
        k_sq = at("k_sq", R[5] + 1088, [P, T])
        k_rs = at("k_rs", R[5] + 2176, [P, T])
        iw_raw = at("iw_raw", R[5] + 3264, [P, TQ])
        relu = [[at(f"relu{a}{t}", R[7] + 1088 * (2 * a + t), [P, T]) for t in range(2)] for a in range(2)]
        score = [at(f"score{t}", R[7] + 4352 + 1088 * t, [P, T]) for t in range(2)]
        top8 = at("top8", R[7] + 6528, [P, 8])
        ki = at("ki", R[7] + 6592, [P, T])
        diff = [at(f"diff{a}", R[5] + 2176 * a, [P, 2 * NC, CH]) for a in range(2)]
        pairs = [at(f"pairs{a}", R[5] + 4352 + 2176 * a, [P, 2 * NC, CH]) for a in range(2)]
        z_att = at("z_att", R[4], [P, 24, T])
        state = at("state", R[7], [P, HEADS, P])
        kv_tok = at("kv_tok", R[7] + 4096, [P, 2, P])
        iq_st = [at(f"iq_st{a}", STG + 1024 * a, [P, SEQ]) for a in range(2)]
        gate_st = [at(f"gate_st{a}", STG + 1032 * a, [P, TQ]) for a in range(2)]
        kv_st = [at(f"kv_st{a}", STG + 2048 * a, [P, 2, HEADS, 32]) for a in range(2)]
        q_st = [at(f"q_st{a}", R[7] + 5120 + 1024 * a, [P, HEADS, CH]) for a in range(2)]
        a_st = [at(f"a_st{a}", R[7] + 5632 + 1024 * a, [P, HEADS, CH]) for a in range(2)]
        qkv_st = at("qkv_st", STG, [P, 3, T])
        probs = at("probs", R[7], [P, 2, T])
        v_keys = at("v_keys", R[7] + 2176, [P, 3, P])
        p_keys = at("p_keys", R[7] + 3712, [P, 2, SEQ])
        p_meta = at("p_meta", R[7] + 5760, [CH, TQ])
        probs2 = at("probs2", R[7] + 6792, [2, CH])
        stat = at("stat", R[7] + 6880, [P, 12])
        ya_hi = at("ya_hi", R[4], [P, HEADS, TQ], F32R)
        ya_lo = at("ya_lo", R[5], [P, HEADS, TQ], F32R)
        z_g = at("z_g", R[3], [P, HEADS, TQ])
        o_sq = at("o_sq", R[0], [P, HEADS, TQ])
        o_rs = at("o_rs", R[1], [P, HEADS, TQ])
        yh_hi = at("yh_hi", R[0], [P, HEADS, TQ], F32R)
        yh_lo = at("yh_lo", R[1], [P, HEADS, TQ], F32R)
        gates = [at(f"gates{a}", R[6] + 2064 * a, [P, 2, TQ]) for a in range(4)]
        h_res = at("h_res", R[0], [P, KT, TQ])
        x_st = [at(f"x_st{a}", R[3] + 3072 * a, [P, 3, 256]) for a in range(2)]
        h_sq = at("h_sq", R[7], [P, TQ])
        ssq = at("ssq", R[7] + 1032, [P, TQ])
        h_rs = at("h_rs", R[7] + 2064, [P, TQ])
        u_tmp = [at(f"u_tmp{a}", R[7] + 3104 + 1032 * a, [P, TQ]) for a in range(2)]
        hid_hi = at("hid_hi", R[0] + 16512, [P, FH, SEQ], F32R)
        hid_lo = at("hid_lo", R[0] + 39040, [P, FH, SEQ], F32R)
        conv = [at(f"conv{a}", R[7] + 5184 + 1024 * a, [P, SEQ]) for a in range(2)]
        f_sq = [at(f"f_sq{a}", R[0] + 16512 + 2048 * a, [P, 2, SEQ]) for a in range(2)]
        f_rs = at("f_rs", R[0] + 16512 + 4096, [P, SEQ])
        out_tok = at("out_tok", R[0] + 24000, [P, 2, D])
        bias = at("bias", BIAS, [P, 2, T])
        bias2 = at("bias2", BIAS + 2176, [2, CH])
        ident = at("ident", CON, [P, P])
        ones = at("ones", CON + 512, [P, P])
        onehot = at("onehot", CON + 1024, [P, 31])
        vec_a = at("vec_a", CON + 1152, [P, V_A])
        vec_b = at("vec_b", CON + 1536, [P, V_B])
        vec_c = at("vec_c", CON + 1888, [P, V_C])
        eps = at("eps", CON + 2144, [P, 1])
        spare = at("spare", CON + 2152, [P, 6])
        lb = at("lb", CON + 2176, [P, 4, HEADS])
        rstat = at("rstat", CON + 2304, [P, 8])
        iw_tok = at("iw_tok", CON + 2336, [P, 2, IDXH])
        keep = at("keep", CON + 2464, [P, T])
        decay = at("decay", CON + 2464, [P, HEADS, NC])

        ps = [ctx.enter_context(nc.psum_tensor(f"ps{i}", [P, 512], F32)) for i in range(8)]
        gate_spill = nc.dram_tensor("gate_spill", (P, 2 * KT, TQ), F32).ap()

        def sem(name):
            return ctx.enter_context(nc.semaphore(name))

        landed = [sem("landed0"), sem("landed1")]
        hi_ready = sem("hi_ready")
        lo_ready = sem("lo_ready")
        projected = sem("projected")
        z_free = sem("z_free")
        gates_free = sem("gates_free")
        merge_free = sem("merge_free")
        out_free = sem("out_free")
        ff_taken = sem("ff_taken")
        down_added = sem("down_added")
        x_in = sem("x_in")
        vec_in = sem("vec_in")
        consts = sem("consts")
        x_sum = sem("x_sum")
        x_var = sem("x_var")
        x_std = sem("x_std")
        x_normed = sem("x_normed")
        x_turned = sem("x_turned")
        uh_ready = sem("uh_ready")
        ul_ready = sem("ul_ready")
        vec_turned = sem("vec_turned")
        vec_ready = sem("vec_ready")
        lb_diff = sem("lb_diff")
        lb_exp = sem("lb_exp")
        key_sq = sem("key_sq")
        key_sum = sem("key_sum")
        key_std = sem("key_std")
        key_ready = sem("key_ready")
        iw_ready = sem("iw_ready")
        iq_staged = sem("iq_staged")
        scored = sem("scored")
        relu_done = sem("relu_done")
        score_added = sem("score_added")
        score_masked = sem("score_masked")
        chosen = sem("chosen")
        bias_ready = sem("bias_ready")
        sig_ready = sem("sig_ready")
        forget_ready = sem("forget_ready")
        log_ready = sem("log_ready")
        scanned = sem("scanned")
        diff_ready = sem("diff_ready")
        decay_ready = sem("decay_ready")
        pair_ready = sem("pair_ready")
        band_used = sem("band_used")
        band_taken = sem("band_taken")
        prep_e = sem("prep_e")
        prep_d = sem("prep_d")
        prep_x = sem("prep_x")
        prep_done = sem("prep_done")
        spill_copied = sem("spill_copied")
        spilled = [sem("spilled0"), sem("spilled1")]
        band_zeroed = sem("band_zeroed")
        band_spread = sem("band_spread")
        pads_zeroed = sem("pads_zeroed")
        staged = sem("staged")
        turned = sem("turned")
        tok_copied = sem("tok_copied")
        step_done = sem("step_done")
        state_ready = sem("state_ready")
        qkv_staged = sem("qkv_staged")
        v_turned = sem("v_turned")
        logits = sem("logits")
        v_copied = sem("v_copied")
        max_ready = sem("max_ready")
        exp_done = sem("exp_done")
        p_ready = sem("p_ready")
        p_turned = sem("p_turned")
        p_copied = sem("p_copied")
        pv_done = sem("pv_done")
        ya_hi_ready = sem("ya_hi_ready")
        ya_ready = sem("ya_ready")
        o_sq_ready = sem("o_sq_ready")
        o_sum = sem("o_sum")
        o_std = sem("o_std")
        o_normed = sem("o_normed")
        g_ready = sem("g_ready")
        o_gated = sem("o_gated")
        yh_hi_ready = sem("yh_hi_ready")
        yh_ready = sem("yh_ready")
        gate_in = [sem(f"gate_in{a}") for a in range(4)]
        gate_sig = sem("gate_sig")
        m_sum = sem("m_sum")
        mh_ready = sem("mh_ready")
        m_ready = sem("m_ready")
        x_st_in = [sem("x_st_in0"), sem("x_st_in1")]
        xt_turned = sem("xt_turned")
        xt_ready = sem("xt_ready")
        ssq_ready = sem("ssq_ready")
        ssq_sum = sem("ssq_sum")
        h_std = sem("h_std")
        u2_ready = sem("u2_ready")
        u2h_ready = sem("u2h_ready")
        u2l_ready = sem("u2l_ready")
        conv_ready = sem("conv_ready")
        silu_ready = sem("silu_ready")
        hid_ready = sem("hid_ready")
        hidh_ready = sem("hidh_ready")
        hidl_ready = sem("hidl_ready")
        f_sq_ready = sem("f_sq_ready")
        f_sum = sem("f_sum")
        f_std = sem("f_std")
        f_ready = sem("f_ready")
        f_turned = sem("f_turned")
        f_copied = sem("f_copied")
        stored = sem("stored")
        pool_step = sem("pool_step")
        dve_step = sem("dve_step")

        block = ctx.enter_context(nc.Block())

        w_cols = w_in[0].rearrange("(k p) n -> p k n", p=P)
        wo_cols = w_out[0].rearrange("(k p) n -> p k n", p=P)
        wg_cols = w_ffn_gate[0].rearrange("(k p) n -> p k n", p=P)
        wu_cols = w_ffn_up[0].rearrange("(k p) n -> p k n", p=P)
        bh_cols = w_branch_hgrn[0].rearrange("(k p) n -> p k n", p=P)
        bd_cols = w_branch_dsa[0].rearrange("(k p) n -> p k n", p=P)
        wd_rows = w_ffn_down[0].rearrange("(k p) n -> p k n", p=P)
        x_rows = x[0].rearrange("(t p) n -> p t n", p=P)

        N_PANELS = U_END // 2
        loads = [3 if p == U_KI // 2 else 2 if U_MERGE <= 2 * p < U_OUT else 1 for p in range(N_PANELS)]
        landed_by = [16 * sum(loads[p % 2:p + 1:2]) for p in range(N_PANELS)]

        @block.sync
        def _(sp):
            sp.dma_start(x_tok[0][0:META, :], meta_tokens).then_inc(x_in, 16)
            for t in range(2):
                sp.dma_start(x_tok[1 + t][:], x_rows[:, t, :]).then_inc(x_in, 16)
            rows = [(0, V_ATTN, attn_norm_w, 16), (0, V_FFN, ffn_norm_w, 16), (0, V_CB, ffn_conv_b, FT),
                    (0, V_LB0, hgrn_lb_logits[0:1, :], 8), (0, V_LB1, hgrn_lb_logits[1:2, :], 8),
                    (0, V_HGN, hgrn_norm_w, 1), (1, V_C0, ffn_conv_w[0, 0:1, :], FT),
                    (1, V_C1, ffn_conv_w[0, 1:2, :], FT), (2, V_C2, ffn_conv_w[0, 2:3, :], FT)]
            for tile, row, src, n in rows:
                sp.dma_start(vec_rows[row:row + n, tile, :],
                             src.rearrange("a (r c) -> (a r) c", c=P)).then_inc(vec_in, 16)
            sp.dma_start(vec_rows[V_FIN:V_FIN + 16, 2, :],
                         final_norm_w.rearrange("(r c) -> r c", c=P)).then_inc(vec_in, 16)
            for half in range(2):
                sp.dma_start(vec_rows[V_IDXK:V_IDXK + 1, 0, 64 * half:64 * half + 64],
                             idx_k_norm_w).then_inc(vec_in, 16)

            def load(p, slot, source, guarded=True):
                if guarded:
                    sp.wait_ge(lo_ready, 2 * p - 2)
                sp.dma_start(raw[slot][:], source).then_inc(landed[slot], 16)

            def columns(first, count, source, c0):
                with sp.Fori(0, count // 2) as i:
                    for b in range(2):
                        load(2 * i + (first + b), (first + b) % 2, source[:, :, ds(512 * i + (c0 + 256 * b), 256)])

            load(0, 0, w_cols[:, :, C_IQ:C_IQ + 256], False)
            load(1, 1, w_cols[:, :, C_IQ + 256:C_IQ + 512], False)
            columns(2, 2, w_cols, C_IQ + 512)
            p = U_KI // 2
            sp.wait_ge(lo_ready, 2 * p - 2)
            for c, src, n in ((0, C_IK, 64), (64, C_IK, 64), (128, C_IW, 16)):
                sp.dma_start(raw[p % 2][:, :, c:c + n], w_cols[:, :, src:src + n]).then_inc(landed[p % 2], 16)
            columns(U_QFI // 2, 12, w_cols, C_HQ)
            columns(U_GATE // 2, 16, w_cols, C_GA)
            columns(U_ATT // 2, 12, w_cols, C_AQ)
            columns(U_G // 2, 4, w_cols, C_HG)
            with sp.Fori(0, 4) as i:
                for b in range(2):
                    p = U_MERGE // 2 + b
                    sp.wait_ge(lo_ready, 4 * i + (2 * p - 2))
                    for branch, src in ((0, bh_cols), (1, bd_cols)):
                        sp.dma_start(raw_b[p % 2][:, branch, :, :], src[:, :, ds(512 * i + 256 * b, 256)])\
                          .then_inc(landed[p % 2], 16)
            columns(U_OUT // 2, 8, wo_cols, 0)
            for half, (u_ff, u_down) in enumerate(((U_FF, U_DOWN), (U_FF2, U_DOWN2))):
                with sp.Fori(0, FH // 2) as i:
                    for b, src in ((0, wg_cols), (1, wu_cols)):
                        load(2 * i + (u_ff // 2 + b), (u_ff // 2 + b) % 2,
                             src[:, :, ds(256 * i + half * FH * P, 256)])

                def down(p, slot, row):
                    sp.wait_ge(lo_ready, 2 * p - 2)
                    sp.dma_start(raw_d[slot], wd_rows[:, row, :]).then_inc(landed[slot], 16)

                first = u_down // 2
                down(first, first % 2, slice(half * FH, half * FH + 2))
                with sp.Fori(0, 5) as i:
                    for b in range(2):
                        down(2 * i + (first + 1 + b), (first + 1 + b) % 2, ds(4 * i + (half * FH + 2 + 2 * b), 2))
            for t in range(2):
                sp.wait_ge(f_copied, 4 * (t + 1))
                sp.dma_start(out[0, P * t:P * t + P, :], out_tok[:, t, :]).then_inc(stored, 16)
            sp.wait_ge(stored, 32)

        @block.gpsimd
        def _(pool):
            steps = Steps(pool_step)
            for tile in (ident, bias2, onehot):
                pool.memset(tile[:], 0.0).then_inc(pool_step, 1)
            pool.memset(ones[:], 1.0).then_inc(consts, 1)
            pool.memset(keep[:], 1.0).then_inc(pool_step, 1)
            pool.memset(eps[:], EPS).then_inc(consts, 1)
            pool.wait_ge(pool_step, 4)
            steps.base = 4
            pool.affine_select(out=ident[:], in_=ident[:], compare_op=ALU.not_equal, fill=1.0, base=0,
                               pattern=[[-1, P]], channel_multiplier=1).then_inc(consts, 1)
            pool.memset(onehot[:, 15:16], 1.0).then_inc(consts, 1)
            pool.memset(keep[:].rearrange("p (c t) -> p c t", t=CH)[:, :, 0:1], 0.0).then_inc(consts, 1)
            pool.affine_select(out=bias2[:], in_=bias2[:], compare_op=ALU.is_ge, fill=-BIG, base=T0,
                               pattern=[[-1, CH]], channel_multiplier=1).then_inc(consts, 1)

            pool.wait_ge(z_free, 8 + 2)
            for j in range(2):
                pool.tensor_copy(iq_st[j][:], iq[:, j, 2:TQ]).then_inc(iq_staged, 1)
            with pool.Fori(1, 4) as i:
                for j in range(2):
                    pool.wait_ge(scored, 4 * i + (2 * j - 2))
                    pool.tensor_copy(iq_st[j][:], iq[:, ds(2 * i + j, 1), 2:TQ].rearrange("p a t -> p (a t)"))\
                        .then_inc(iq_staged, 1)
            pool.wait_ge(score_added, IDXH + 2)
            for t in range(2):
                pool.affine_select(out=score[t][:], in_=score[t][:], compare_op=ALU.is_ge, fill=FUTURE,
                                   base=META + P * t, pattern=[[-1, T]], channel_multiplier=1)\
                    .then_inc(score_masked, 1)
            for t in range(2):
                pool.wait_ge(chosen, t + 1)
                pool.affine_select(out=bias[:, t, :], in_=bias[:, t, :], compare_op=ALU.is_ge, fill=-BIG,
                                   base=META + P * t, pattern=[[-1, T]], channel_multiplier=1)\
                    .then_inc(bias_ready, 1)

            pool.memset(band[:], 0.0).then_inc(band_zeroed, 1)
            pool.wait_ge(band_zeroed, 1)
            pool.wait_ge(band_taken, 5)
            for j in range(4):
                pool.dma_start(band[32 * j:32 * j + CH, :, :].rearrange("s (a j) t -> s j a t", j=4)[:, j, :, :],
                               band_rows[:].rearrange("s (a j) t -> s j a t", j=4)[:, j, :, :])\
                    .then_inc(band_spread, 16)
            pool.wait_ge(spilled[0], 16 * 16)
            pool.wait_ge(spilled[1], 16 * 16)
            for tile in kv_st:
                pool.memset(tile[:], 0.0).then_inc(pads_zeroed, 1)
            pool.wait_ge(pads_zeroed, 2)
            pool.wait_ge(prep_done, 4)

            def stage(c, slot):
                tok = ds(c * CH, CH)
                pool.tensor_copy(kv_st[slot][:, 0, :, 0:CH], z_k[:, :, tok]).then_inc(staged, 1)
                pool.tensor_copy(kv_st[slot][:, 1, :, 0:CH], z_v[:, :, tok]).then_inc(staged, 1)
                pool.tensor_copy(q_st[slot][:], z_q[:, :, tok]).then_inc(staged, 1)
                if isinstance(c, int) and c == 0:
                    pool.wait_ge(band_spread, 64)
                pool.tensor_copy(a_st[slot][:], band[:, :, tok]).then_inc(staged, 1)

            for c in range(2):
                stage(c, c)
            with pool.Fori(1, 8) as i:
                for b in range(2):
                    pool.wait_ge(step_done, 4 * i + (2 * b - 2))
                    stage(2 * i + b, b)
            pool.wait_ge(step_done, 2 * (NC - 1) - 2)
            stage(NC - 1, (NC - 1) % 2)

            def stage_head(h):
                for n in range(3):
                    pool.tensor_copy(qkv_st[:, n, :], z_att[:, ds(h + 8 * n, 1), :].rearrange("p a t -> p (a t)"))\
                        .then_inc(qkv_staged, 1)

            pool.wait_ge(step_done, 2 * NC)
            pool.wait_ge(z_free, U_G - 32 + 2)
            stage_head(0)
            with pool.Fori(1, 8) as h:
                pool.wait_ge(logits, h)
                stage_head(h)

            def gate_pair(n, slot):
                pool.dma_start(gates[slot][:], gate_spill[:, :, :].rearrange("p (g k) t -> p g k t", g=2)
                               [:, :, n, :]).then_inc(gate_in[slot], 16)

            pool.wait_ge(qkv_staged, 3 * HEADS)
            for n in range(4):
                gate_pair(n, n)
            with pool.Fori(1, 4) as i:
                for a in range(4):
                    pool.wait_ge(m_ready, 4 * i + (a - 3))
                    pool.dma_start(gates[a][:], gate_spill[:, :, :].rearrange("p (g k) t -> p g k t", g=2)
                                   [:, :, ds(4 * i + a, 1), :].rearrange("p g k t -> p g (k t)"))\
                        .then_inc(gate_in[a], 16)

            def x_panel(slot, cols):
                pool.dma_start(x_st[slot][:, 1:3, :], x_rows[:, :, cols]).then_inc(x_st_in[slot], 16)
                pool.dma_start(x_st[slot][0:META, 0, :], meta_tokens[:, cols]).then_inc(x_st_in[slot], 16)

            def squares(n, tile, last=False):
                pool.wait_ge(out_free, n + 3)
                src = h_res[:, tile, :].rearrange("p a t -> p (a t)")
                steps.link(pool, pool.tensor_tensor(h_sq[:], src, src, ALU.mult))
                ins = pool.tensor_tensor(ssq[:], ssq[:], h_sq[:], ALU.add)
                if last:
                    ins.then_inc(ssq_ready, 1)
                else:
                    steps.link(pool, ins)

            pool.wait_ge(o_gated, HEADS)
            steps.link(pool, pool.memset(ssq[:], 0.0))
            for b in range(2):
                x_panel(b, slice(256 * b, 256 * b + 256))
            with pool.Fori(0, 3) as i:
                steps.enter(i, 8)
                for b in range(2):
                    pool.wait_ge(xt_turned, 4 * i + (2 * b + 2))
                    x_panel(b, ds(512 * i + (512 + 256 * b), 256))
                    for a in range(2):
                        squares(4 * i + (2 * b + a), ds(4 * i + (2 * b + a), 1))
            steps.leave(3)
            for n in range(12, 16):
                squares(n, slice(n, n + 1), n == 15)

        @block.tensor
        def _(pe):
            mm = nc.tensor.matmul

            def products(acc, s, ks, mov_hi, mov_lo, wk=None, first=0, last=KT - 1):
                for k in ks:
                    mm(acc, w_hi[s][:, k, :], mov_hi(k), start=(k == first), stop=False)
                    mm(acc, w_hi[s][:, k, :], mov_lo(k), start=False, stop=False)
                    ins = mm(acc, w_lo[s][:, k, :], mov_hi(k), start=False, stop=(k == last))
                return ins

            def tokens(t0, hi=u_hi, lo=u_lo, end=T):
                return lambda k: hi[:, k, t0:end], lambda k: lo[:, k, t0:end]

            def project(n, s, bank, t0, parts=((0, KT),), between=()):
                pe.wait_ge(lo_ready, n + 1)
                for q, (a, b) in enumerate(parts):
                    ins = products(ps[bank][:, 0:T - t0], s, range(a, b), *tokens(t0))
                    if q == len(parts) - 1:
                        ins.then_inc(projected, 1)
                    if q < len(between):
                        between[q]()

            pe.wait_ge(consts, 6)
            pe.wait_ge(vec_in, 16 * 12)
            for n, rows in enumerate((V_A, V_B, V_C)):
                ins = nc.tensor.transpose(ps[5 + n][:, 0:rows], vec_rows[0:rows, n, :], ident[0:rows, 0:rows])
            ins.then_inc(vec_turned, 1)
            pe.wait_ge(x_normed, 3)
            for k in range(KT):
                if k >= 4:
                    pe.wait_ge(ul_ready, k - 3)
                cols = slice(P * k, P * k + P)
                nc.tensor.transpose(ps[k % 4][:, 0:META], x_tok[0][0:META, cols], ident[0:META, 0:META])
                for t in range(2):
                    ins = nc.tensor.transpose(ps[k % 4][:, META + P * t:META + P * t + P], x_tok[1 + t][:, cols],
                                              ident[:])
                ins.then_inc(x_turned, 1)
            pe.wait_ge(ul_ready, KT)

            with pe.Fori(0, 2) as i:
                for u in range(4):
                    pe.wait_ge(z_free, 4 * i + (u + 1))
                    project(4 * i + u, u, u % 2, T0)
            pe.wait_ge(z_free, 9)
            project(8, 0, 0, 0)
            pe.wait_ge(z_free, 10)
            project(9, 1, 1, T0)
            pe.wait_ge(key_sq, 1)
            mm(ps[2][:, 0:T], ones[:], k_sq[:], start=True, stop=True).then_inc(key_sum, 1)
            pe.wait_ge(z_free, 12)
            for t in range(2):
                ins = nc.tensor.transpose(ps[3][:, 16 * t:16 * t + 16], iw_raw[0:IDXH, 2 + P * t:2 + P * t + P],
                                          ident[0:IDXH, 0:IDXH])
            ins.then_inc(iw_ready, 1)

            pe.wait_ge(key_ready, 2)
            with pe.Fori(0, 4) as i:
                for u in range(4):
                    pe.wait_ge(iq_staged, 2 * i + (u // 2 + 1))
                    pe.wait_ge(relu_done, 8 * i + (2 * u + 2))
                    half = slice(64 * (u % 2), 64 * (u % 2) + 64)
                    for t in range(2):
                        ins = mm(ps[2 + 2 * (u % 2) + t][:, 0:T], iq_st[u // 2][half, P * t:P * t + P], ki[half, :],
                                 start=True, stop=True)
                    ins.then_inc(scored, 1)
                    n = U_QFI + u
                    pe.wait_ge(z_free, 4 * i + (n + 1))
                    project(4 * i + n, n % 4, n % 2, 0)
            with pe.Fori(0, 2) as i:
                for u in range(4):
                    n = U_QFI + 16 + u
                    pe.wait_ge(z_free, 4 * i + (n + 1))
                    project(4 * i + n, n % 4, n % 2, 0)

            pe.wait_ge(z_free, U_GATE + 2)
            with pe.Fori(0, 4) as i:
                for u in range(8):
                    n = U_GATE + u
                    pe.wait_ge(gates_free, 8 * i + (u + 1))
                    project(8 * i + n, n % 4, n % 2, T0)
                    if u == 0:
                        pe.wait_ge(band_taken, i + 1)
                    for s in (2 * u, 2 * u + 1):
                        pe.wait_ge(pair_ready, 16 * i + (s + 1))
                        for a in range(2):
                            o = ps[2 + a][0:CH, 0:T].rearrange("p (c t) -> p c t", t=CH)[:, :, s:CH]
                            r = pairs[s % 2][:, NC * a:NC * a + NC, s:CH]
                            ins = mm(o, onehot[:, 15 - s:31 - s], r, start=(s == 0), stop=(s == CH - 1))
                        ins.then_inc(band_used, 1)

            def turn(slot, h0, wait_stage):
                pe.wait_ge(staged, wait_stage)
                for n in range(2):
                    ins = nc.tensor.transpose(ps[2][:, P * n:P * n + P],
                                              kv_st[slot][:, n, h0:h0 + 4, :].rearrange("p h t -> p (h t)"), ident[:])
                ins.then_inc(turned, 1)

            def step(k, slot, h0, update=True):
                pe.wait_ge(tok_copied, k + 1)
                pe.wait_ge(state_ready, k + 2)
                o = ps[5][:, 0:4 * CH]
                mm(o, kv_tok[:, 1, :], a_st[slot][:, h0:h0 + 4, :].rearrange("p h t -> p (h t)"),
                   start=True, stop=False, skip_group_check=True)
                for j in range(4):
                    ins = mm(o[:, CH * j:CH * j + CH], state[:, h0 + j, :], q_st[slot][:, h0 + j, :],
                             start=False, stop=True, skip_group_check=True)
                if update:
                    for j in range(4):
                        tok = slice(32 * j, 32 * j + CH)
                        ins = mm(ps[UPDATE_BANKS[j]][:, 0:P], kv_tok[tok, 0, :], kv_tok[tok, 1, :],
                                 start=True, stop=True)
                ins.then_inc(step_done, 1)

            def half_chunk(i, k):
                c = k // 2
                return 16 * i + k, c % 2, 4 * (k % 2), 32 * i + 4 * (c + 1)

            when = ([(1, 4), (12, 16)], [(8, 12)], [(5, 9)])
            pe.wait_ge(gates_free, 32 + 2)
            with pe.Fori(0, 2) as i:
                for u in range(12):
                    n = U_ATT + u
                    pe.wait_ge(z_free, 12 * i + (n - 32 + 1))
                    cuts, jobs = [0], []
                    for j, (t_turn, t_step) in enumerate(when[u % 3]):
                        kk, slot, h0, st = half_chunk(i, 4 * (u // 3) + (0, 2, 3)[u % 3] + j)
                        cuts += [t_turn, t_step]
                        jobs += [lambda a=(slot, h0, st): turn(*a), lambda a=(kk, slot, h0): step(*a)]
                    if cuts[-1] < KT:
                        cuts.append(KT)
                    project(12 * i + n, n % 4, n % 2, 0, tuple(zip(cuts, cuts[1:])), jobs)
            for k in (32, 33):
                turn(0, 4 * (k % 2), 4 * NC)
                step(k, 0, 4 * (k % 2), False)

            pe.wait_ge(o_sq_ready, 2)
            for h in range(HEADS):
                if h >= 6:
                    pe.wait_ge(o_std, h - 5)
                mm(ps[2 + h % 6][:, 0:TQ], ones[:], o_sq[:, h, :], start=True, stop=True).then_inc(o_sum, 1)
            pe.wait_ge(o_std, HEADS)

            with pe.Fori(0, 2) as i:
                for u in range(4):
                    pe.wait_ge(qkv_staged, 12 * i + 3 * (u + 1))
                    for m, (a, b) in enumerate(((0, META), (META, META + P), (META + P, T))):
                        ins = nc.tensor.transpose(ps[6][0:b - a, P * m:P * m + P], qkv_st[:, 2, a:b], ident[:])
                    ins.then_inc(v_turned, 1)
                    for t in range(2):
                        mm(ps[4 + t][:, 0:T], qkv_st[:, 0, META + P * t:META + P * t + P], qkv_st[:, 1, :],
                           start=True, stop=True)
                    mm(ps[4][0:2, T:T + CH], qkv_st[:, 0, T0:META], qkv_st[:, 1, 0:CH],
                       start=True, stop=True).then_inc(logits, 1)

                    def turn_p(i=i, u=u):
                        pe.wait_ge(p_ready, 4 * i + (u + 1))
                        pe.wait_ge(v_copied, 8 * i + 2 * (u + 1))
                        for t in range(2):
                            nc.tensor.transpose(ps[7][0:CH, 2 + P * t:2 + P * t + P], probs[:, t, 0:META], ident[:])
                            for m in range(2):
                                nc.tensor.transpose(ps[6][:, SEQ * m + P * t:SEQ * m + P * t + P],
                                                    probs[:, t, META + P * m:META + P * m + P], ident[:])
                        nc.tensor.transpose(ps[7][0:CH, 0:2], probs2[:], ident[0:2, 0:2]).then_inc(p_turned, 1)

                    def values(i=i, u=u):
                        pe.wait_ge(p_copied, 8 * i + 2 * (u + 1))
                        pe.wait_ge(ya_ready, 4 * i + (u + 1))
                        mm(ps[2][:, 0:TQ], v_keys[0:CH, 0, :], p_meta[:], start=True, stop=False)
                        mm(ps[2][:, 2:TQ], v_keys[:, 1, :], p_keys[:, 0, :], start=False, stop=False)
                        mm(ps[2][:, 2:TQ], v_keys[:, 2, :], p_keys[:, 1, :], start=False, stop=True)\
                            .then_inc(pv_done, 1)

                    n = U_G + u
                    pe.wait_ge(z_free, 4 * i + (n - 32 + 1))
                    project(4 * i + n, n % 4, n % 2, T0, ((0, 13), (13, KT)), (turn_p, values))

            pe.wait_ge(z_free, U_MERGE - 32 + 2)
            pe.wait_ge(ya_ready, 9)
            with pe.Fori(0, 4) as i:
                for u in range(4):
                    n = U_MERGE + u
                    pe.wait_ge(lo_ready, 4 * i + (n + 1))
                    pe.wait_ge(merge_free, 4 * i + (u + 1))
                    s, bank = n % 4, 2 * (u % 2)
                    products(ps[bank + 1][:, 0:TQ], s, range(8, 16), lambda k: ya_hi[:, k - 8, :],
                             lambda k: ya_lo[:, k - 8, :], first=8, last=15)
                    for k in range(8):
                        if u == 0:
                            pe.wait_ge(yh_ready, k + 1)
                        ins = products(ps[bank][:, 0:TQ], s, (k,), lambda k: yh_hi[:, k, :],
                                       lambda k: yh_lo[:, k, :], last=7)
                    ins.then_inc(projected, 1)

            pe.wait_ge(merge_free, 18)
            pe.wait_ge(m_ready, 16)
            with pe.Fori(0, 4) as i:
                for u in range(4):
                    n = U_OUT + u
                    if u % 2 == 0:
                        pe.wait_ge(x_st_in[u // 2], 32 * i + 32)
                    pe.wait_ge(out_free, 4 * i + (u + 1))
                    bank = 2 + u % 2
                    for t in range(2):
                        nc.tensor.transpose(ps[bank][:, META + P * t:META + P * t + P],
                                            x_st[u // 2][:, 1 + t, P * (u % 2):P * (u % 2) + P], ident[:])
                    nc.tensor.transpose(ps[bank][:, 0:META], x_st[u // 2][0:META, 0, P * (u % 2):P * (u % 2) + P],
                                        ident[0:META, 0:META]).then_inc(xt_turned, 1)
                    pe.wait_ge(lo_ready, 4 * i + (n + 1))
                    products(ps[u % 2][:, 0:TQ], n % 4, range(KT), lambda k: m_hi[:, k, :], lambda k: m_lo[:, k, :])\
                        .then_inc(projected, 1)
            pe.wait_ge(ssq_ready, 1)
            mm(ps[4][:, 0:TQ], ones[:], ssq[:], start=True, stop=True).then_inc(ssq_sum, 1)

            for half, (u_ff, u_down) in enumerate(((U_FF, U_DOWN), (U_FF2, U_DOWN2))):
                if half == 0:
                    pe.wait_ge(out_free, 18)
                else:
                    pe.wait_ge(down_added, 4)
                with pe.Fori(0, FH // 2) as i:
                    for u in range(4):
                        n = u_ff + u
                        t0, cols = (0, TQ) if u < 2 else (2, SEQ)
                        pe.wait_ge(lo_ready, 4 * i + (n + 1))
                        pe.wait_ge(ff_taken, 4 * i + (2 * FH * half + u + 1))
                        for k in range(KT):
                            if half == 0 and u == 0:
                                pe.wait_ge(u2l_ready, k + 1)
                            ins = products(ps[4 * half + u][:, 0:cols], n % 4, (k,), *tokens(t0, m_hi, m_lo, TQ))
                        ins.then_inc(projected, 1)

                def down(n, s, u, tile, half=half):
                    pe.wait_ge(lo_ready, n + 1)
                    first = isinstance(tile, int) and tile == 0
                    for kk in range(2):
                        t = tile + kk
                        mh, ml = ((hid_hi[:, t, :], hid_lo[:, t, :]) if first else
                                  (hid_hi[:, ds(t, 1), :].rearrange("p a t -> p (a t)"),
                                   hid_lo[:, ds(t, 1), :].rearrange("p a t -> p (a t)")))
                        for g in range(8):
                            acc = ps[4 * ((u + half + 1) % 2) + g // 2][:, SEQ * (g % 2):SEQ * (g % 2) + SEQ]
                            w = 8 * kk + g
                            mm(acc, w_hi[s][:, w, :], mh, start=(first and kk == 0 and g % 2 == 0), stop=False,
                               skip_group_check=True)
                            mm(acc, w_hi[s][:, w, :], ml, start=False, stop=False, skip_group_check=True)
                            ins = mm(acc, w_lo[s][:, w, :], mh, start=False, stop=True, skip_group_check=True)
                    ins.then_inc(projected, 1)

                if half == 1:
                    pe.wait_ge(down_added, 8)
                pe.wait_ge(hidl_ready, FH * half + 2)
                down(u_down, u_down % 4, 0, 0)
                pe.wait_ge(ff_taken, 2 * FH * (half + 1) + 4)
                down(u_down + 1, (u_down + 1) % 4, 1, 0)
                pe.wait_ge(hidl_ready, FH * (half + 1))
                with pe.Fori(0, 5) as i:
                    for u in range(4):
                        n = u_down + 2 + u
                        down(4 * i + n, n % 4, u % 2, 4 * i + (2 + 2 * (u // 2)))

            for b in range(8):
                pe.wait_ge(f_sq_ready, b + 1)
                if b == 0:
                    pe.wait_ge(down_added, 16)
                for a in range(2):
                    ins = mm(ps[0][:, 0:SEQ], ones[:], f_sq[b % 2][:, a, :], start=(b + a == 0), stop=(b + a == 8))
                ins.then_inc(f_sum, 1)
            for t in range(2):
                for j in range(4):
                    pe.wait_ge(f_ready, 4 * (j + 1))
                    bank = 4 * t + j
                    if bank == 0:
                        pe.wait_ge(f_std, 1)
                    for k in range(4 * j, 4 * j + 4):
                        ins = nc.tensor.transpose(ps[bank][:, P * (k % 4):P * (k % 4) + P],
                                                  h_res[:, k, 2 + P * t:2 + P * t + P], ident[:])
                    ins.then_inc(f_turned, 1)

        @block.scalar
        def _(act):
            activation = nc.scalar.activation

            def settle():
                act.wait_ge(consts, 6)

            def round_unit(n, m, landed_at):
                if m > 3:
                    act.wait_ge(projected, n - 3)
                if m % 2 == 0:
                    act.wait_ge(landed[(m // 2) % 2], landed_at)
                activation(w_hi[m % 4][:], raw[(m // 2) % 2][:, :, P * (m % 2):P * (m % 2) + P], ACT.Copy)\
                    .then_inc(hi_ready, 1)

            def ahead(n):
                if n + 3 < U_END:
                    round_unit(n + 3, n + 3, landed_by[(n + 3) // 2])

            def pace(n0, per, times):
                out = []
                for u in range(per):
                    units = [n0 + 3 + u + per * t for t in range(times)]
                    if units[-1] >= U_END:
                        return None
                    at = [landed_by[m // 2] for m in units]
                    grows = {b - a for a, b in zip(at, at[1:])}
                    if len(grows) > 1:
                        return None
                    out.append(grows.pop())
                return out

            def loop(n0, per, times, body, early=0):
                full = times
                while full > 1 and pace(n0 + early, per, full) is None:
                    full -= 1
                if full > 1:
                    grows = pace(n0 + early, per, full)
                    with act.Fori(0, full) as i:
                        for u in range(per):
                            m = n0 + early + u + 3
                            body(i, u, lambda m=m, g=grows[u]: round_unit(per * i + m, m, g * i + landed_by[m // 2]))
                for i in range(full if full > 1 else 0, times):
                    for u in range(per):
                        body(i, u, lambda n=n0 + early + per * i + u: ahead(n))

            act.wait_ge(consts, 6)
            activation(spare[:, 0:1], eps[:], ACT.Copy).then_inc(gates_free, 2)
            activation(spare[:, 1:2], eps[:], ACT.Copy).then_inc(relu_done, 4)
            act.wait_ge(z_free, 2)
            act.wait_ge(x_in, 48)
            for t, rows in enumerate((META, P, P)):
                activation(junk[0:rows, :], x_tok[t][0:rows, :], ACT.Square,
                           accum_out=rstat[0:rows, t:t + 1]).then_inc(x_sum, 1)
                if t < 2:
                    act.wait_ge(x_sum, t + 1)
            act.wait_ge(x_sum, 3)
            activation(rstat[:, 3:6], rstat[:, 0:3], ACT.Sqrt, bias=eps[:], scale=1.0 / D).then_inc(x_std, 1)
            for m in range(3):
                round_unit(m, m, landed_by[m // 2])
            act.wait_ge(vec_ready, 3)
            for k in range(KT):
                act.wait_ge(x_turned, k + 1)
                activation(u_hi[:, k, :], ps[k % 4][:, 0:T], ACT.Copy, scale=vec_a[:, V_ATTN + k:V_ATTN + k + 1])\
                    .then_inc(uh_ready, 1)
            act.wait_ge(lb_diff, 1)
            activation(lb[:, 1:3, :], lb[:, 1:3, :], ACT.Exp).then_inc(lb_exp, 1)

            for n in range(9):
                ahead(n)
            act.wait_ge(z_free, 8 + 1 + 2)
            activation(k_sq[:], k_raw[:], ACT.Square).then_inc(key_sq, 1)
            act.wait_ge(key_sum, 1)
            activation(k_rs[:], ps[2][:, 0:T], ACT.Sqrt, bias=eps[:], scale=1.0 / P).then_inc(key_std, 1)
            ahead(9)

            def score_unit(i, u, split):
                act.wait_ge(scored, 4 * i + (u + 1))
                act.wait_ge(score_added, 4 * i + (u + 1))
                for t in range(2):
                    activation(relu[u % 2][t][:], ps[2 + 2 * (u % 2) + t][:, 0:T], ACT.Relu).then_inc(relu_done, 1)
                split()

            loop(U_QFI, 4, 4, score_unit)
            for u in range(8):
                n = U_QFI + 16 + u
                ahead(n)
                if u == 1:
                    act.wait_ge(z_free, U_QFI + 16 + 2)
                    activation(sig[:], z_k[:], ACT.Sigmoid).then_inc(sig_ready, 1)
                    act.wait_ge(sig_ready, 1)
                    activation(z_k[:], z_k[:], ACT.Sigmoid, scale=-1.0).then_inc(sig_ready, 1)
                if u == 2:
                    activation(z_q[:], z_q[:], ACT.Silu).then_inc(sig_ready, 1)
                if u == 5:
                    act.wait_ge(forget_ready, 1)
                    activation(z_b[:], sig[:], ACT.Ln).then_inc(log_ready, 1)

            def decays(i, u):
                for s in (2 * u, 2 * u + 1):
                    act.wait_ge(diff_ready, 16 * i + (s + 1))
                    activation(diff[s % 2][:, :, s:CH], diff[s % 2][:, :, s:CH], ACT.Exp).then_inc(decay_ready, 1)

            def gate_unit(i, u, split):
                if u == 0:
                    decays(i, 0)
                split()
                if u < 7:
                    decays(i, u + 1)
                b = u % 2
                if u >= 2:
                    act.wait_ge(spilled[b], 64 * i + 16 * (u // 2))
                act.wait_ge(projected, 8 * i + (U_GATE + u + 1))
                activation(gate_st[b][:], ps[(U_GATE + u) % 2][:, 0:TQ], ACT.Copy).then_inc(gates_free, 1)
                act.wait_ge(gates_free, 8 * i + (u + 3))
                act.dma_start(gate_spill[:, ds(8 * i + u, 1), :].rearrange("p a t -> p (a t)"), gate_st[b][:])\
                    .then_inc(spilled[b], 16)
                if u == 7:
                    act.wait_ge(pair_ready, 16 * i + 16)
                    settle()
                    zb = z_b[:].rearrange("p h t -> p (h t)")[:, ds(2 * T * i, 2 * T)]
                    activation(diff[0][:].rearrange("p c t -> p (c t)"), zb, ACT.Exp).then_inc(prep_e, 1)
                    act.wait_ge(prep_d, i + 1)
                    dec = decay[:].rearrange("p h c -> p (h c)")[:, ds(2 * NC * i, 2 * NC)]
                    activation(dec, dec, ACT.Exp).then_inc(prep_x, 1)
                    activation(diff[1][:].rearrange("p c t -> p (c t)"), zb, ACT.Exp).then_inc(prep_x, 1)
                    for q in range(2):
                        act.wait_ge(spilled[q], 64 * i + 64)

            loop(U_GATE, 8, 4, gate_unit)

            def copy_tok(k):
                act.wait_ge(turned, k + 1)
                activation(kv_tok[:].rearrange("p a b -> p (a b)"), ps[2][:, 0:2 * P], ACT.Copy).then_inc(tok_copied, 1)

            def att_unit(i, u, split):
                k = 4 * (u // 3) + (0, 2, 3)[u % 3]
                if u % 3 == 0:
                    copy_tok(16 * i + k)
                    split()
                    copy_tok(16 * i + (k + 1))
                else:
                    split()
                    copy_tok(16 * i + k)

            loop(U_ATT, 12, 2, att_unit)
            act.wait_ge(staged, 4 * NC)
            act.wait_ge(state_ready, 2 * (NC - 1) + 2)
            edge = T - CH
            copy_tok(32)
            activation(o_sq[:, :, 0:edge - T0], z_v[:, :, T0:edge], ACT.Square).then_inc(o_sq_ready, 1)
            copy_tok(33)
            act.wait_ge(state_ready, 2 * NC + 2)
            activation(o_sq[:, :, edge - T0:TQ], z_v[:, :, edge:T], ACT.Square).then_inc(o_sq_ready, 1)
            for h in range(HEADS):
                act.wait_ge(o_sum, h + 1)
                activation(o_rs[:, h, :], ps[2 + h % 6][:, 0:TQ], ACT.Sqrt, bias=eps[:], scale=1.0 / P)\
                    .then_inc(o_std, 1)

            def head_unit(i, u, split):
                h1 = 4 * i + (u + 1)
                act.wait_ge(v_turned, h1)
                activation(v_keys[0:CH, 0, :], ps[6][0:CH, 0:P], ACT.Copy).then_inc(v_copied, 1)
                activation(v_keys[:, 1:3, :], ps[6][:, P:3 * P].rearrange("p (a b) -> p a b", a=2), ACT.Copy)\
                    .then_inc(v_copied, 1)
                act.wait_ge(max_ready, h1)
                for t in range(2):
                    activation(probs[:, t, :], probs[:, t, :], ACT.Exp, bias=stat[:, t:t + 1],
                               accum_out=stat[:, 4 + t:5 + t]).then_inc(exp_done, 1)
                activation(probs2[:], probs2[:], ACT.Exp, bias=stat[0:2, 2:3], accum_out=stat[0:2, 6:7])\
                    .then_inc(exp_done, 1)
                split()
                act.wait_ge(p_turned, h1)
                activation(p_keys[:].rearrange("p a b -> p (a b)"), ps[6][:], ACT.Copy).then_inc(p_copied, 1)
                activation(p_meta[:], ps[7][0:CH, 0:TQ], ACT.Copy).then_inc(p_copied, 1)
                act.wait_ge(pv_done, h1)
                settle()
                activation(ya_hi[:, ds(4 * i + u, 1), :].rearrange("p a t -> p (a t)"), ps[2][:, 0:TQ], ACT.Copy)\
                    .then_inc(ya_hi_ready, 1)

            loop(U_G, 4, 2, head_unit)

            act.wait_ge(z_free, U_MERGE - 32 + 2)
            for h in range(HEADS + 1):
                if h < HEADS:
                    activation(z_g[:, h, :], z_g[:, h, :], ACT.Silu).then_inc(g_ready, 1)
                if h:
                    act.wait_ge(o_gated, h)
                    activation(yh_hi[:, h - 1, :], z_v[:, h - 1, T0:T], ACT.Copy).then_inc(yh_hi_ready, 1)

            def merge_unit(i, u, split):
                act.wait_ge(gate_in[u], 16 * i + 16)
                activation(gates[u][:], gates[u][:], ACT.Sigmoid).then_inc(gate_sig, 1)
                split()
                act.wait_ge(m_sum, 4 * i + (u + 1))
                settle()
                activation(m_hi[:, ds(4 * i + u, 1), :].rearrange("p a t -> p (a t)"), gates[u][:, 0, :], ACT.Copy)\
                    .then_inc(mh_ready, 1)

            ahead(U_MERGE)
            loop(U_MERGE, 4, 4, merge_unit, early=1)

            def out_unit(i, u, split):
                act.wait_ge(xt_turned, 4 * i + (u + 1))
                settle()
                activation(h_res[:, ds(4 * i + u, 1), :].rearrange("p a t -> p (a t)"), ps[2 + u % 2][:, T0:T],
                           ACT.Copy).then_inc(xt_ready, 1)
                split()

            loop(U_OUT, 4, 4, out_unit, early=1)
            act.wait_ge(ssq_sum, 1)
            activation(h_rs[:], ps[4][:, 0:TQ], ACT.Sqrt, bias=eps[:], scale=1.0 / D).then_inc(h_std, 1)
            with act.Fori(0, KT // 2) as i:
                for b in range(2):
                    act.wait_ge(u2_ready, 2 * i + (b + 1))
                    settle()
                    activation(m_hi[:, ds(2 * i + b, 1), :].rearrange("p a t -> p (a t)"), u_tmp[b][:], ACT.Copy)\
                        .then_inc(u2h_ready, 1)

            for half, (u_ff, u_down) in enumerate(((U_FF, U_DOWN), (U_FF2, U_DOWN2))):
                def ff_unit(i, u, split, half=half):
                    split()
                    if u < 2:
                        act.wait_ge(ff_taken, 4 * i + (2 * FH * half + u + 5))
                        activation(conv[u][:], conv[u][:], ACT.Silu).then_inc(silu_ready, 1)
                    else:
                        a = u - 2
                        act.wait_ge(ff_taken, 4 * i + (2 * FH * half + u + 5))
                        settle()
                        activation(hid_hi[:, ds(2 * i + a, 1), :].rearrange("p a t -> p (a t)"), conv[a][:], ACT.Copy)\
                            .then_inc(hidh_ready, 1)

                if half == 1:
                    ahead(u_ff)
                loop(u_ff, 4, FH // 2, ff_unit, early=1)
                ahead(u_down + 1)
                loop(u_down + 2, 4, 5, lambda i, u, split: split())

            for b in range(8):
                act.wait_ge(down_added, 8 + b + 1)
                if b >= 2:
                    act.wait_ge(f_sum, b - 1)
                act_in = h_res[:].rearrange("p (g u) t -> p u g t", u=2)[:, b // 4, 2 * (b % 4):2 * (b % 4) + 2, 2:TQ]
                activation(f_sq[b % 2][:], act_in, ACT.Square).then_inc(f_sq_ready, 1)
            act.wait_ge(f_sum, 8)
            activation(f_rs[:], ps[0][:, 0:SEQ], ACT.Sqrt, bias=eps[:], scale=1.0 / D).then_inc(f_std, 1)
            for t in range(2):
                for j in range(4):
                    act.wait_ge(f_turned, 4 * t + j + 1)
                    activation(out_tok[:, t, 512 * j:512 * j + 512], ps[4 * t + j][:], ACT.Copy).then_inc(f_copied, 1)

        @block.vector
        def _(dve):
            v = nc.vector
            steps = Steps(dve_step)
            link = lambda ins: steps.link(dve, ins)

            def rest(n, m):
                dve.wait_ge(hi_ready, n + 1)
                v.tensor_tensor(w_lo[m % 4][:], raw[(m // 2) % 2][:, :, P * (m % 2):P * (m % 2) + P],
                                w_hi[m % 4][:].bitcast(F32), ALU.subtract).then_inc(lo_ready, 1)

            def ahead(n, m):
                if isinstance(n, int) and n + 3 >= U_END:
                    return
                rest(n + 3, m + 3)

            v.memset(rstat[:], 1.0).then_inc(z_free, 2)
            v.memset(lb[:], 0.0).then_inc(ff_taken, 4)
            v.memset(spare[:, 2:3], 0.0).then_inc(merge_free, 2)
            v.memset(spare[:, 3:4], 0.0).then_inc(out_free, 2)
            v.memset(spare[:, 4:5], 0.0).then_inc(band_taken, 1)
            dve.wait_ge(vec_turned, 1)
            for n, (dst, cols) in enumerate(((vec_a, V_A), (vec_b, V_B), (vec_c, V_C))):
                v.tensor_copy(dst[:], ps[5 + n][:, 0:cols]).then_inc(vec_ready, 1)
            dve.wait_ge(x_sum, 3)
            dve.wait_ge(x_std, 1)
            link(v.reciprocal(rstat[:, 0:3], rstat[:, 3:6]))
            for t, rows in enumerate((META, P, P)):
                v.tensor_scalar(x_tok[t][0:rows, :], x_tok[t][0:rows, :], rstat[0:rows, t:t + 1], None, ALU.mult)\
                    .then_inc(x_normed, 1)
            dve.wait_ge(vec_ready, 3)
            link(v.tensor_tensor(lb[:, 0, :], vec_a[:, V_LB0:V_LB0 + 8], vec_a[:, V_LB1:V_LB1 + 8], ALU.max))
            v.tensor_tensor(lb[:, 1, :], vec_a[:, V_LB0:V_LB0 + 8], lb[:, 0, :], ALU.subtract)
            v.tensor_tensor(lb[:, 2, :], vec_a[:, V_LB1:V_LB1 + 8], lb[:, 0, :], ALU.subtract).then_inc(lb_diff, 1)
            for m in range(3):
                rest(m, m)
            for k in range(KT):
                dve.wait_ge(uh_ready, k + 1)
                v.scalar_tensor_tensor(u_lo[:, k, :], ps[k % 4][:, 0:T], vec_a[:, V_ATTN + k:V_ATTN + k + 1],
                                       u_hi[:, k, :].bitcast(F32), ALU.mult, ALU.subtract).then_inc(ul_ready, 1)
            dve.wait_ge(lb_exp, 1)
            link(v.tensor_tensor(lb[:, 0, :], lb[:, 1, :], lb[:, 2, :], ALU.add))
            link(v.reciprocal(lb[:, 0, :], lb[:, 0, :]))
            v.tensor_tensor(lb[:, 3, :], lb[:, 2, :], lb[:, 0, :], ALU.mult)
            link(v.tensor_tensor(lb[:, 1, :], lb[:, 1, :], lb[:, 0, :], ALU.mult))

            with dve.Fori(0, 2) as i:
                for u in range(4):
                    ahead(4 * i + u, u)
                    dve.wait_ge(projected, 4 * i + (u + 1))
                    v.tensor_copy(iq[:, ds(4 * i + u, 1), :].rearrange("p a t -> p (a t)"), ps[u % 2][:, 0:TQ])\
                        .then_inc(z_free, 1)
            dve.wait_ge(projected, 9)
            v.tensor_copy(k_raw[:], ps[0][:, 0:T]).then_inc(z_free, 1)
            ahead(8, 8)
            dve.wait_ge(projected, 10)
            v.tensor_copy(iw_raw[0:IDXH, :], ps[1][0:IDXH, 0:TQ]).then_inc(z_free, 1)
            dve.wait_ge(key_std, 1)
            link(v.reciprocal(k_rs[:], k_rs[:]))
            v.scalar_tensor_tensor(ki[:], k_raw[:], vec_a[:, V_IDXK:V_IDXK + 1], k_rs[:], ALU.mult, ALU.mult)\
                .then_inc(key_ready, 1)
            dve.wait_ge(iw_ready, 1)
            v.tensor_scalar(iw_tok[:].rearrange("p a b -> p (a b)"), ps[3][:, 0:32],
                            (IDXH ** -0.5) * (64 ** -0.5), None, ALU.mult).then_inc(key_ready, 1)
            v.memset(score[0][:], 0.0)
            v.memset(score[1][:], 0.0).then_inc(score_added, 2)
            ahead(9, 9)

            with dve.Fori(0, 4) as i:
                for u in range(4):
                    m = U_QFI + u
                    dve.wait_ge(relu_done, 8 * i + (2 * u + 2 + 4))
                    dve.wait_ge(score_added, 4 * i + (u + 2))
                    for t in range(2):
                        ins = v.scalar_tensor_tensor(score[t][:], relu[u % 2][t][:],
                                                     iw_tok[:, t, ds(4 * i + u, 1)], score[t][:], ALU.mult, ALU.add)
                    ins.then_inc(score_added, 1)
                    ahead(4 * i + m, m)
                    dve.wait_ge(projected, 4 * i + (m + 1))
                    v.tensor_copy(z_qf[:, ds(4 * i + u, 1), :].rearrange("p a t -> p (a t)"), ps[m % 2][:, 0:T])\
                        .then_inc(z_free, 1)

            def top_keys(t, rounds):
                for r in range(rounds):
                    link(v.max(top8[:], score[t][:]))
                    link(v.match_replace(score[t][:], top8[:], score[t][:], TAKEN))

            for u in range(8):
                m = U_QFI + 16 + u
                if u == 0:
                    dve.wait_ge(score_masked, 2)
                if u < 4:
                    top_keys(u // 2, 4)
                    if u % 2:
                        t = u // 2
                        link(v.tensor_scalar(bias[:, t, :], score[t][:], TAKEN, BIG, ALU.is_equal, ALU.mult))
                        v.tensor_scalar(bias[:, t, :], bias[:, t, :], -BIG, None, ALU.add).then_inc(chosen, 1)
                if u == 4:
                    dve.wait_ge(sig_ready, 2)
                    for h in range(HEADS):
                        v.tensor_scalar(z_k[:, h, :], z_k[:, h, :], lb[:, 3, h:h + 1], None, ALU.mult)
                        ins = v.tensor_scalar(sig[:, h, :], sig[:, h, :], lb[:, 3, h:h + 1], lb[:, 1, h:h + 1],
                                              ALU.mult, ALU.add)
                    ins.then_inc(forget_ready, 1)
                if u == 6:
                    dve.wait_ge(log_ready, 1)
                    for h in range(HEADS):
                        ins = v.tensor_tensor_scan(z_b[:, h, :], keep[:], z_b[:, h, :], 0.0, ALU.mult, ALU.add)
                    link(ins)
                ahead(m, m)
                dve.wait_ge(projected, m + 1)
                v.tensor_copy(z_v[:, u, :], ps[m % 2][:, 0:T]).then_inc(z_free, 1)

            zf = lambda z, i: z[:].rearrange("p h t -> p (h t)")[:, ds(2 * T * i, 2 * T)]\
                .rearrange("p (c t) -> p c t", t=CH)

            def differences(i, u):
                for s in (2 * u, 2 * u + 1):
                    v.tensor_tensor(diff[s % 2][:, :, s:CH], zf(z_b, i)[:, :, s:CH],
                                    zf(z_b, i)[:, :, s:s + 1].to_broadcast([P, 2 * NC, CH - s]), ALU.subtract)\
                        .then_inc(diff_ready, 1)

            dve.wait_ge(sig_ready, 3)
            with dve.Fori(0, 4) as i:
                steps.enter(i, 17)
                for u in range(8):
                    m = U_GATE + u
                    if u == 0:
                        differences(i, 0)
                    for s in (2 * u, 2 * u + 1):
                        w = CH - s
                        dve.wait_ge(decay_ready, 16 * i + (s + 1))
                        link(v.tensor_tensor(diff[s % 2][:, :, s:CH], diff[s % 2][:, :, s:CH],
                                             zf(z_k, i)[:, :, s:s + 1].to_broadcast([P, 2 * NC, w]), ALU.mult))
                        if s >= 2:
                            dve.wait_ge(band_used, 16 * i + (s - 1))
                        v.tensor_tensor(pairs[s % 2][:, :, s:CH], diff[s % 2][:, :, s:CH],
                                        zf(z_q, i)[:, :, s:CH], ALU.mult).then_inc(pair_ready, 1)
                    if u < 7:
                        dve.wait_ge(pair_ready, 16 * i + 2 * (u + 1))
                        differences(i, u + 1)
                    ahead(8 * i + m, m)
                dve.wait_ge(band_used, 16 * i + 16)
                for a in range(2):
                    ins = v.tensor_copy(band_rows[:, ds(2 * i + a, 1), :].rearrange("p a t -> p (a t)"),
                                        ps[2 + a][0:CH, 0:T])
                ins.then_inc(band_taken, 1)
                dec = decay[:].rearrange("p h c -> p (h c)")[:, ds(2 * NC * i, 2 * NC)]\
                    .rearrange("p (c a) -> p c a", a=1)
                link(v.tensor_copy(dec, zf(z_b, i)[:, :, CH - 1:CH]))
                dve.wait_ge(prep_e, i + 1)
                v.tensor_tensor(zf(z_b, i), dec.to_broadcast([P, 2 * NC, CH]), zf(z_b, i), ALU.subtract)\
                    .then_inc(prep_d, 1)
                v.tensor_tensor(zf(z_q, i), zf(z_q, i), diff[0][:], ALU.mult)
                dve.wait_ge(prep_x, 2 * i + 2)
                v.tensor_tensor(zf(z_k, i), zf(z_k, i), diff[1][:], ALU.mult).then_inc(prep_done, 1)
                dve.wait_ge(prep_done, i + 1)
            steps.leave(4)

            v.memset(state[:], 0.0).then_inc(state_ready, 2)

            def advance(k, c, h0, update=True):
                dve.wait_ge(step_done, k + 1)
                o = v.tensor_copy(z_v[:, h0:h0 + 4, ds(c * CH, CH)],
                                  ps[5][:, 0:4 * CH].rearrange("p (h t) -> p h t", h=4))
                if not update:
                    o.then_inc(state_ready, 1)
                    return
                s = state[:, h0:h0 + 4, :]
                link(v.tensor_tensor(s, s, decay[:, h0:h0 + 4, ds(c, 1)].to_broadcast([P, 4, P]), ALU.mult))
                for j in range(4):
                    ins = v.tensor_tensor(state[:, h0 + j, :], ps[UPDATE_BANKS[j]][:, 0:P], state[:, h0 + j, :], ALU.add)
                ins.then_inc(state_ready, 1)

            with dve.Fori(0, 2) as i:
                steps.enter(i, 16)
                for u in range(12):
                    m = U_ATT + u
                    k = 4 * (u // 3) + (0, 2, 3)[u % 3]
                    ahead(12 * i + m, m)
                    advance(16 * i + k, 8 * i + k // 2, 4 * (k % 2))
                    dve.wait_ge(projected, 12 * i + (m + 1))
                    v.tensor_copy(z_att[:, ds(12 * i + u, 1), :].rearrange("p a t -> p (a t)"), ps[m % 2][:, 0:T])\
                        .then_inc(z_free, 1)
                    if u % 3 == 0:
                        advance(16 * i + k + 1, 8 * i + (k + 1) // 2, 4 * ((k + 1) % 2))
            steps.leave(2)
            for k in (32, 33):
                advance(k, 16, 4 * (k % 2), False)

            dve.wait_ge(bias_ready, 2)
            link(v.memset(stat[:], 1.0))
            v.memset(stat[:, 3:4], 0.0).then_inc(ya_ready, 1)
            dve.wait_ge(o_std, HEADS)
            with dve.Fori(0, 2) as i:
                steps.enter(i, 16)
                for u in range(4):
                    m = U_G + u
                    dve.wait_ge(logits, 4 * i + (u + 1))
                    for t in range(2):
                        v.scalar_tensor_tensor(probs[:, t, :], ps[4 + t][:, 0:T], SCALE, bias[:, t, :],
                                               ALU.mult, ALU.add)
                    link(v.scalar_tensor_tensor(probs2[:], ps[4][0:2, T:T + CH], SCALE, bias2[:], ALU.mult, ALU.add))
                    v.tensor_reduce(stat[:, 0:2], probs[:], AX.X, ALU.max)
                    link(v.tensor_reduce(stat[0:2, 2:3], probs2[:], AX.X, ALU.max))
                    v.tensor_scalar(stat[:, 0:3], stat[:, 0:3], -1.0, None, ALU.mult).then_inc(max_ready, 1)
                    dve.wait_ge(exp_done, 12 * i + 3 * (u + 1))
                    link(v.reciprocal(stat[:, 8:11], stat[:, 4:7]))
                    for t in range(2):
                        v.tensor_scalar(probs[:, t, :], probs[:, t, :], stat[:, 8 + t:9 + t], None, ALU.mult)
                    v.tensor_scalar(probs2[:], probs2[:], stat[0:2, 10:11], None, ALU.mult).then_inc(p_ready, 1)
                    ahead(4 * i + m, m)
                    h = ds(4 * i + u, 1)
                    rs = o_rs[:, h, :].rearrange("p a t -> p (a t)")
                    o = z_v[:, h, T0:T].rearrange("p a t -> p (a t)")
                    link(v.reciprocal(rs, rs))
                    v.scalar_tensor_tensor(o, o, vec_a[:, V_HGN:V_HGN + 1], rs, ALU.mult, ALU.mult)\
                        .then_inc(o_normed, 1)
                    dve.wait_ge(projected, 4 * i + (m + 1))
                    v.tensor_copy(z_g[:, ds(4 * i + u, 1), :].rearrange("p a t -> p (a t)"), ps[m % 2][:, 0:TQ])\
                        .then_inc(z_free, 1)
                    dve.wait_ge(ya_hi_ready, 4 * i + (u + 1))
                    v.tensor_tensor(ya_lo[:, h, :].rearrange("p a t -> p (a t)"), ps[2][:, 0:TQ],
                                    ya_hi[:, h, :].rearrange("p a t -> p (a t)").bitcast(F32), ALU.subtract)\
                        .then_inc(ya_ready, 1)
            steps.leave(2)

            dve.wait_ge(o_normed, HEADS)
            for h in range(HEADS + 1):
                if h < HEADS:
                    o = z_v[:, h, T0:T]
                    dve.wait_ge(g_ready, h + 1)
                    v.tensor_tensor(o, o, z_g[:, h, :], ALU.mult).then_inc(o_gated, 1)
                if h:
                    dve.wait_ge(yh_hi_ready, h)
                    v.tensor_tensor(yh_lo[:, h - 1, :], z_v[:, h - 1, T0:T], yh_hi[:, h - 1, :].bitcast(F32),
                                    ALU.subtract).then_inc(yh_ready, 1)
            ahead(U_MERGE, U_MERGE)

            with dve.Fori(0, 4) as i:
                for u in range(4):
                    m = U_MERGE + u
                    dve.wait_ge(projected, 4 * i + (m + 1))
                    dve.wait_ge(gate_sig, 4 * i + (u + 1))
                    bank = 2 * (u % 2)
                    v.tensor_tensor(gates[u][:, 0, :], ps[bank][:, 0:TQ], gates[u][:, 0, :], ALU.mult)
                    v.tensor_tensor(gates[u][:, 1, :], ps[bank + 1][:, 0:TQ], gates[u][:, 1, :], ALU.mult)\
                        .then_inc(merge_free, 1)
                    dve.wait_ge(merge_free, 4 * i + (u + 3))
                    v.tensor_tensor(gates[u][:, 0, :], gates[u][:, 0, :], gates[u][:, 1, :], ALU.add)\
                        .then_inc(m_sum, 1)
                    ahead(4 * i + (m + 1), m + 1)
                    dve.wait_ge(mh_ready, 4 * i + (u + 1))
                    t = ds(4 * i + u, 1)
                    v.tensor_tensor(m_lo[:, t, :].rearrange("p a t -> p (a t)"), gates[u][:, 0, :],
                                    m_hi[:, t, :].rearrange("p a t -> p (a t)").bitcast(F32), ALU.subtract)\
                        .then_inc(m_ready, 1)

            with dve.Fori(0, 4) as i:
                for u in range(4):
                    m = U_OUT + u
                    dve.wait_ge(projected, 4 * i + (m + 1))
                    dve.wait_ge(xt_ready, 4 * i + (u + 1))
                    h = h_res[:, ds(4 * i + u, 1), :].rearrange("p a t -> p (a t)")
                    v.tensor_tensor(h, ps[u % 2][:, 0:TQ], h, ALU.add).then_inc(out_free, 1)
                    ahead(4 * i + (m + 1), m + 1)

            dve.wait_ge(h_std, 1)
            dve.wait_ge(out_free, 18)
            link(v.reciprocal(h_rs[:], h_rs[:]))

            def scale(k, b, vec=None):
                v.scalar_tensor_tensor(u_tmp[b][:], h_res[:, k, :].rearrange("p a t -> p (a t)"), vec_a[:, vec], h_rs[:],
                                       ALU.mult, ALU.mult).then_inc(u2_ready, 1)

            def low_part(k, n, b):
                dve.wait_ge(u2h_ready, n + 1)
                v.tensor_tensor(m_lo[:, k, :].rearrange("p a t -> p (a t)"), u_tmp[b][:],
                                m_hi[:, k, :].rearrange("p a t -> p (a t)").bitcast(F32), ALU.subtract)\
                    .then_inc(u2l_ready, 1)

            scale(slice(0, 1), 0, slice(V_FFN, V_FFN + 1))
            scale(slice(1, 2), 1, slice(V_FFN + 1, V_FFN + 2))
            with dve.Fori(0, KT // 2 - 1) as i:
                for b in range(2):
                    low_part(ds(2 * i + b, 1), 2 * i + b, b)
                    dve.wait_ge(u2l_ready, 2 * i + (b + 1))
                    scale(ds(2 * i + (b + 2), 1), b, ds(2 * i + (V_FFN + b + 2), 1))
            for b in range(2):
                low_part(slice(KT - 2 + b, KT - 1 + b), KT - 2 + b, b)

            for half, (u_ff, u_down) in enumerate(((U_FF, U_DOWN), (U_FF2, U_DOWN2))):
                if half == 1:
                    ahead(u_ff, u_ff)
                with dve.Fori(0, FH // 2) as i:
                    steps.enter(i, 4)

                    def low(a):
                        dve.wait_ge(hidh_ready, 2 * i + (FH * half + a + 1))
                        j = ds(2 * i + a, 1)
                        v.tensor_tensor(hid_lo[:, j, :].rearrange("p a t -> p (a t)"), conv[a][:],
                                        hid_hi[:, j, :].rearrange("p a t -> p (a t)").bitcast(F32), ALU.subtract)\
                            .then_inc(hidl_ready, 1)

                    for u in range(4):
                        m = u_ff + u
                        if u == 3:
                            low(0)
                        dve.wait_ge(projected, 4 * i + (m + 1))
                        if u < 2:
                            tap = lambda vec, c: vec[:, ds(2 * i + (c + FH * half + u), 1)]
                            c = conv[u][:]
                            bank = ps[4 * half + u]
                            link(v.tensor_scalar(c, bank[:, 2:TQ], tap(vec_c, V_C2), tap(vec_a, V_CB),
                                                 ALU.mult, ALU.add))
                            link(v.scalar_tensor_tensor(c, bank[:, 1:TQ - 1], tap(vec_b, V_C1), c, ALU.mult, ALU.add))
                            v.scalar_tensor_tensor(c, bank[:, 0:TQ - 2], tap(vec_b, V_C0), c, ALU.mult, ALU.add)\
                                .then_inc(ff_taken, 1)
                        else:
                            c = conv[u - 2][:]
                            dve.wait_ge(silu_ready, 2 * i + (FH * half + u - 1))
                            v.tensor_tensor(c, ps[4 * half + u][:, 0:SEQ], c, ALU.mult).then_inc(ff_taken, 1)
                        ahead(4 * i + (m + 1), m + 1)
                    low(1)
                steps.leave(FH // 2)

                ahead(u_down + 1, u_down + 1)
                with dve.Fori(0, 4) as i:
                    for u in range(4):
                        ahead(4 * i + (u_down + 2 + u), u_down + 2 + u)
                for n in range(u_down + 18, u_down + FH):
                    ahead(n, n)
                for b in range(8):
                    if b % 4 == 0:
                        dve.wait_ge(projected, u_down + FH - 1 + b // 4)
                    h = h_res[:].rearrange("p (g u) t -> p u g t", u=2)[:, b // 4, 2 * (b % 4):2 * (b % 4) + 2, 2:TQ]
                    bank = ps[(b + 4 * (half + 1)) % 8]
                    v.tensor_tensor(h, bank[:].rearrange("p (g t) -> p g t", g=2), h, ALU.add).then_inc(down_added, 1)

            dve.wait_ge(f_std, 1)
            link(v.reciprocal(f_rs[:], f_rs[:]))
            for k in range(KT):
                v.scalar_tensor_tensor(h_res[:, k, 2:TQ], h_res[:, k, 2:TQ], vec_c[:, V_FIN + k:V_FIN + k + 1],
                                       f_rs[:], ALU.mult, ALU.mult).then_inc(f_ready, 1)


_INS = ['x', 'meta_tokens', 'attn_norm_w', 'w_in', 'hgrn_lb_logits', 'hgrn_norm_w', 'idx_k_norm_w',
        'w_branch_hgrn', 'w_branch_dsa', 'w_out', 'ffn_norm_w', 'w_ffn_gate', 'w_ffn_up',
        'ffn_conv_w', 'ffn_conv_b', 'w_ffn_down', 'final_norm_w']


def kernel(**inputs):
    import numpy as np
    import concourse.bacc as bacc
    from concourse.bass_utils import run_bass_kernel_spmd as run

    nc = bacc.Bacc("TRN2", target_bir_lowering=False, num_devices=1)
    arrays, args = {}, []
    for name in _INS:
        a = np.ascontiguousarray(inputs[name])
        arrays[f"in_{name}_dram"] = a
        args.append(nc.dram_tensor(f"in_{name}_dram", a.shape, mybir.dt.from_np(a.dtype), kind="ExternalInput").ap())
    args.append(nc.dram_tensor("out_0_dram", (1, SEQ, D), F32, kind="ExternalOutput").ap())
    hybrid_block(nc, *args)
    r = run(nc, [arrays], core_ids=[0])
    return r.results[0]["out_0_dram"]
```

```python
from contextlib import ExitStack

import concourse.bass as bass
from concourse import mybir

F32 = mybir.dt.float32
F32R = mybir.dt.float32r
ACT = mybir.ActivationFunctionType
ALU = mybir.AluOpType
AX = mybir.AxisListType
ds = bass.ds

P = 128
D = 2048
KT = D // P
META, SEQ = 16, 256
T = META + SEQ
T0 = META - 2
TQ = T - T0
HEADS = 8
FF = 5632
FT = FF // P
FH = FT // 2
CH = 16
NC = T // CH
IDXH = 16
TOPK = 64
EPS = 1e-6
SCALE = float(P) ** -0.5
BIG = 2.0 ** 100
FUTURE = -2.0 ** 126
TAKEN = -2.0 ** 127

U_IQ = 0
U_KI = U_IQ + 8
U_QFI = U_KI + 2
U_GATE = U_QFI + 24
U_ATT = U_GATE + 32
U_G = U_ATT + 24
U_MERGE = U_G + 8
U_OUT = U_MERGE + 16
U_FF = U_OUT + 16
U_DOWN = U_FF + 2 * FH
U_FF2 = U_DOWN + FH
U_DOWN2 = U_FF2 + 2 * FH
U_END = U_DOWN2 + FH
C_HQ, C_HG, C_AQ, C_IQ, C_IK, C_IW, C_GA, C_GB = 0, 3072, 4096, 7168, 8192, 8256, 8272, 10320

V_ATTN, V_FFN, V_LB0, V_LB1, V_HGN, V_IDXK, V_CB = 0, 16, 32, 40, 48, 49, 50
V_A = 94
V_C0, V_C1, V_B = 0, 44, 88
V_C2, V_FIN, V_C = 0, 44, 60

K_POOL = 11
UPDATE_BANKS = (3, 4, 6, 7)
ZB = HEADS * T * 4


class Steps:

    def __init__(self, sem):
        self.sem, self.base, self.per, self.i, self.j = sem, 0, 0, None, 0

    def enter(self, i, per):
        self.base, self.i, self.per, self.j = self.base + self.j, i, per, 0

    def leave(self, times):
        assert self.j == self.per, (self.j, self.per)
        self.base, self.i, self.j = self.base + self.per * times, None, 0

    def value(self):
        return self.base + self.j if self.i is None else self.i * self.per + (self.base + self.j)

    def link(self, eng, ins):
        ins.then_inc(self.sem, 1)
        self.j += 1
        eng.wait_ge(self.sem, self.value())


def hybrid_block(nc, x, meta_tokens, attn_norm_w, w_in, hgrn_lb_logits, hgrn_norm_w, idx_k_norm_w,
                 w_branch_hgrn, w_branch_dsa, w_out, ffn_norm_w, w_ffn_gate, w_ffn_up,
                 ffn_conv_w, ffn_conv_b, w_ffn_down, final_norm_w, out):
    ctx = ExitStack()
    with ctx:
        SLAB = 212832
        ctx.enter_context(nc.sbuf_tensor("slab", [P, SLAB // 4], F32))
        ORIGIN = 16512

        def at(name, offset, shape, dt=F32):
            size = 4
            for n in shape[1:]:
                size *= n
            assert offset + size <= SLAB, (name, offset + size)
            return nc.alloc_sbuf_tensor_at(name, shape, dt, offset=ORIGIN + offset, align_bytes=8)

        raw = [at(f"raw{i}", 16384 * i, [P, KT, 256]) for i in range(2)]
        raw_b = [t[:].rearrange("p (b k) c -> p b k c", b=2) for t in raw]
        raw_d = [t[:].rearrange("p (a g) c -> p a (g c)", a=2) for t in raw]
        w_hi = [at(f"w_hi{i}", 32768 + 8192 * i, [P, KT, P], F32R) for i in range(4)]
        w_lo = [at(f"w_lo{i}", 65536 + 8192 * i, [P, KT, P], F32R) for i in range(4)]
        UA = 98304
        u_hi = at("u_hi", UA, [P, KT, T], F32R)
        u_lo = at("u_lo", UA + 17408, [P, KT, T], F32R)
        m_hi = at("m_hi", UA, [P, KT, TQ], F32R)
        m_lo = at("m_lo", UA + 17408, [P, KT, TQ], F32R)
        R = [133120 + ZB * j for j in range(9)]
        BIAS = R[8]
        STG = BIAS + 2304
        CON = STG + 4112

        x_tok = [at(f"x_tok{i}", R[0] + 8192 * i, [P, D]) for i in range(3)]
        junk = at("junk", R[0] + 24576, [P, D])
        vec_rows = at("vec_rows", R[7], [P, 3, P])
        z_qf = at("z_qf", R[0], [P, 2 * HEADS, T])
        z_q, z_k = z_qf[:, 0:HEADS, :], z_qf[:, HEADS:2 * HEADS, :]
        z_v = at("z_v", R[2], [P, HEADS, T])
        band = at("band", R[3], [P, HEADS, T])
        band_rows = at("band_rows", R[6], [CH, HEADS, T])
        z_b = at("z_b", R[4], [P, HEADS, T])
        sig = at("sig", R[5], [P, HEADS, T])
        iq = at("iq", R[6], [P, 8, TQ])
        k_raw = at("k_raw", R[5], [P, T])
        k_sq = at("k_sq", R[5] + 1088, [P, T])
        k_rs = at("k_rs", R[5] + 2176, [P, T])
        iw_raw = at("iw_raw", R[5] + 3264, [P, TQ])
        relu = [[at(f"relu{a}{t}", R[7] + 1088 * (2 * a + t), [P, T]) for t in range(2)] for a in range(2)]
        score = [at(f"score{t}", R[7] + 4352 + 1088 * t, [P, T]) for t in range(2)]
        top8 = at("top8", R[7] + 6528, [P, 8])
        ki = at("ki", R[7] + 6592, [P, T])
        diff = [at(f"diff{a}", R[5] + 2176 * a, [P, 2 * NC, CH]) for a in range(2)]
        pairs = [at(f"pairs{a}", R[5] + 4352 + 2176 * a, [P, 2 * NC, CH]) for a in range(2)]
        z_att = at("z_att", R[4], [P, 24, T])
        state = at("state", R[7], [P, HEADS, P])
        kv_tok = at("kv_tok", R[7] + 4096, [P, 2, P])
        iq_st = [at(f"iq_st{a}", STG + 1024 * a, [P, SEQ]) for a in range(2)]
        gate_st = [at(f"gate_st{a}", R[7] + 5120 + 1032 * a, [P, TQ]) for a in range(2)]
        kv_tok2 = at("kv_tok2", R[7] + 7184, [P, 2, P])
        kv_st = [at(f"kv_st{a}", STG + 2048 * a, [P, 2, HEADS, 32]) for a in range(2)]
        q_st = [at(f"q_st{a}", R[7] + 5120 + 1024 * a, [P, HEADS, CH]) for a in range(2)]
        a_st = [at(f"a_st{a}", R[7] + 5632 + 1024 * a, [P, HEADS, CH]) for a in range(2)]
        qkv_st = at("qkv_st", STG, [P, 3, T])
        probs = at("probs", R[7], [P, 2, T])
        v_keys = at("v_keys", R[7] + 2176, [P, 3, P])
        p_keys = at("p_keys", R[7] + 3712, [P, 2, SEQ])
        p_meta = at("p_meta", R[7] + 5760, [CH, TQ])
        probs2 = at("probs2", R[7] + 6792, [2, CH])
        stat = at("stat", R[7] + 6880, [P, 12])
        ya_hi = at("ya_hi", R[4], [P, HEADS, TQ], F32R)
        ya_lo = at("ya_lo", R[5], [P, HEADS, TQ], F32R)
        z_g = at("z_g", R[3], [P, HEADS, TQ])
        o_sq = at("o_sq", R[0], [P, HEADS, TQ])
        o_rs = at("o_rs", R[1], [P, HEADS, TQ])
        yh_hi = at("yh_hi", R[0], [P, HEADS, TQ], F32R)
        yh_lo = at("yh_lo", R[1], [P, HEADS, TQ], F32R)
        gates = [at(f"gates{a}", R[6] + 2064 * a, [P, 2, TQ]) for a in range(4)]
        h_res = at("h_res", R[0], [P, KT, TQ])
        x_st = [at(f"x_st{a}", R[3] + 3072 * a, [P, 3, 256]) for a in range(2)]
        h_sq = at("h_sq", R[7], [P, TQ])
        ssq = at("ssq", R[7] + 1032, [P, TQ])
        h_rs = at("h_rs", R[7] + 2064, [P, TQ])
        u_tmp = [at(f"u_tmp{a}", R[5] + 1032 * a, [P, TQ]) for a in range(4)]
        hid_hi = at("hid_hi", R[0] + 16512, [P, FH, SEQ], F32R)
        hid_lo = at("hid_lo", R[0] + 39040, [P, FH, SEQ], F32R)
        conv = [at(f"conv{a}", R[7] + 5184 + 1024 * a, [P, SEQ]) for a in range(2)]
        f_sq = [at(f"f_sq{a}", R[0] + 16512 + 2048 * a, [P, 2, SEQ]) for a in range(8)]
        f_rs = at("f_rs", R[0] + 16512 + 16384, [P, SEQ])
        out_tok = at("out_tok", R[4], [P, 2, D])
        bias = at("bias", BIAS, [P, 2, T])
        bias2 = at("bias2", BIAS + 2176, [2, CH])
        ident = at("ident", CON, [P, P])
        ones = at("ones", CON + 512, [P, P])
        onehot = at("onehot", CON + 1024, [P, 31])
        vec_a = at("vec_a", CON + 1152, [P, V_A])
        vec_b = at("vec_b", CON + 1536, [P, V_B])
        vec_c = at("vec_c", CON + 1888, [P, V_C])
        eps = at("eps", CON + 2144, [P, 1])
        spare = at("spare", CON + 2152, [P, 6])
        lb = at("lb", CON + 2176, [P, 4, HEADS])
        rstat = at("rstat", CON + 2304, [P, 8])
        iw_tok = at("iw_tok", CON + 2336, [P, 2, IDXH])
        keep = at("keep", CON + 2464, [P, T])
        decay = at("decay", CON + 2464, [P, HEADS, NC])

        ps = [ctx.enter_context(nc.psum_tensor(f"ps{i}", [P, 512], F32)) for i in range(8)]
        gate_spill = nc.dram_tensor("gate_spill", (P, 2 * KT, TQ), F32).ap()

        def sem(name):
            return ctx.enter_context(nc.semaphore(name))

        landed = [sem("landed0"), sem("landed1")]
        hi_ready = sem("hi_ready")
        lo_ready = sem("lo_ready")
        projected = sem("projected")
        z_free = sem("z_free")
        gates_free = sem("gates_free")
        merge_free = sem("merge_free")
        out_free = sem("out_free")
        ff_taken = sem("ff_taken")
        down_added = sem("down_added")
        x_in = [sem(f"x_in{t}") for t in range(3)]
        vec_in = sem("vec_in")
        consts = sem("consts")
        x_sum = sem("x_sum")
        x_rstd = sem("x_rstd")
        x_std = sem("x_std")
        x_normed = sem("x_normed")
        x_turned = sem("x_turned")
        uh_ready = sem("uh_ready")
        ul_ready = sem("ul_ready")
        vec_turned = sem("vec_turned")
        vec_ready = sem("vec_ready")
        lb_diff = sem("lb_diff")
        lb_exp = sem("lb_exp")
        key_sq = sem("key_sq")
        key_sum = sem("key_sum")
        key_std = sem("key_std")
        key_ready = sem("key_ready")
        iw_ready = sem("iw_ready")
        iq_staged = sem("iq_staged")
        scored = sem("scored")
        relu_done = sem("relu_done")
        score_added = sem("score_added")
        score_masked = sem("score_masked")
        chosen = sem("chosen")
        bias_ready = sem("bias_ready")
        sig_ready = sem("sig_ready")
        forget_ready = sem("forget_ready")
        log_ready = sem("log_ready")
        scanned = sem("scanned")
        diff_ready = sem("diff_ready")
        decay_ready = sem("decay_ready")
        pair_ready = sem("pair_ready")
        band_used = sem("band_used")
        band_taken = sem("band_taken")
        prep_e = sem("prep_e")
        prep_d = sem("prep_d")
        prep_x = sem("prep_x")
        prep_done = sem("prep_done")
        spill_copied = sem("spill_copied")
        spilled = [sem("spilled0"), sem("spilled1")]
        band_zeroed = sem("band_zeroed")
        band_spread = sem("band_spread")
        pads_zeroed = sem("pads_zeroed")
        staged = sem("staged")
        turned = sem("turned")
        tok_copied = sem("tok_copied")
        step_done = sem("step_done")
        state_ready = sem("state_ready")
        qkv_staged = sem("qkv_staged")
        v_turned = sem("v_turned")
        logits = sem("logits")
        v_copied = sem("v_copied")
        max_ready = sem("max_ready")
        exp_done = sem("exp_done")
        p_ready = sem("p_ready")
        p_turned = sem("p_turned")
        p_copied = sem("p_copied")
        pv_done = sem("pv_done")
        ya_hi_ready = sem("ya_hi_ready")
        ya_ready = sem("ya_ready")
        o_sq_ready = sem("o_sq_ready")
        o_sum = sem("o_sum")
        o_std = sem("o_std")
        o_rsqrt = sem("o_rsqrt")
        o_normed = sem("o_normed")
        g_ready = sem("g_ready")
        o_gated = sem("o_gated")
        yh_hi_ready = sem("yh_hi_ready")
        yh_ready = sem("yh_ready")
        gate_in = [sem(f"gate_in{a}") for a in range(4)]
        gate_sig = sem("gate_sig")
        m_sum = sem("m_sum")
        mh_ready = sem("mh_ready")
        m_ready = sem("m_ready")
        x_st_in = [sem("x_st_in0"), sem("x_st_in1")]
        xt_turned = sem("xt_turned")
        xt_ready = sem("xt_ready")
        ssq_ready = sem("ssq_ready")
        ssq_sum = sem("ssq_sum")
        h_std = sem("h_std")
        u2_ready = sem("u2_ready")
        u2h_ready = sem("u2h_ready")
        u2l_ready = sem("u2l_ready")
        conv_ready = sem("conv_ready")
        silu_ready = sem("silu_ready")
        hid_ready = sem("hid_ready")
        hidh_ready = sem("hidh_ready")
        hidl_ready = sem("hidl_ready")
        f_sq_ready = sem("f_sq_ready")
        f_rs_ready = sem("f_rs_ready")
        f_pool_ready = sem("f_pool_ready")
        f_half = sem("f_half")
        f_weighted = sem("f_weighted")
        f_sum = sem("f_sum")
        f_std = sem("f_std")
        f_ready = sem("f_ready")
        f_turned = sem("f_turned")
        f_copied = sem("f_copied")
        stored = sem("stored")
        pool_step = sem("pool_step")
        dve_step = sem("dve_step")

        block = ctx.enter_context(nc.Block())

        w_cols = w_in[0].rearrange("(k p) n -> p k n", p=P)
        wo_cols = w_out[0].rearrange("(k p) n -> p k n", p=P)
        wg_cols = w_ffn_gate[0].rearrange("(k p) n -> p k n", p=P)
        wu_cols = w_ffn_up[0].rearrange("(k p) n -> p k n", p=P)
        bh_cols = w_branch_hgrn[0].rearrange("(k p) n -> p k n", p=P)
        bd_cols = w_branch_dsa[0].rearrange("(k p) n -> p k n", p=P)
        wd_rows = w_ffn_down[0].rearrange("(k p) n -> p k n", p=P)
        x_rows = x[0].rearrange("(t p) n -> p t n", p=P)

        N_PANELS = U_END // 2
        loads = [3 if p == U_KI // 2 else 2 if U_MERGE <= 2 * p < U_OUT else 1 for p in range(N_PANELS)]
        landed_by = [16 * sum(loads[p % 2:p + 1:2]) for p in range(N_PANELS)]

        @block.sync
        def _(sp):
            sp.dma_start(x_tok[0][0:META, :], meta_tokens).then_inc(x_in[0], 16)
            for t in range(2):
                sp.dma_start(x_tok[1 + t][:], x_rows[:, t, :]).then_inc(x_in[1 + t], 16)
            rows = [(0, V_ATTN, attn_norm_w, 16), (0, V_FFN, ffn_norm_w, 16), (0, V_CB, ffn_conv_b, FT),
                    (0, V_LB0, hgrn_lb_logits[0:1, :], 8), (0, V_LB1, hgrn_lb_logits[1:2, :], 8),
                    (0, V_HGN, hgrn_norm_w, 1), (1, V_C0, ffn_conv_w[0, 0:1, :], FT),
                    (1, V_C1, ffn_conv_w[0, 1:2, :], FT), (2, V_C2, ffn_conv_w[0, 2:3, :], FT)]
            for tile, row, src, n in rows:
                sp.dma_start(vec_rows[row:row + n, tile, :],
                             src.rearrange("a (r c) -> (a r) c", c=P)).then_inc(vec_in, 16)
            sp.dma_start(vec_rows[V_FIN:V_FIN + 16, 2, :],
                         final_norm_w.rearrange("(r c) -> r c", c=P)).then_inc(vec_in, 16)
            for half in range(2):
                sp.dma_start(vec_rows[V_IDXK:V_IDXK + 1, 0, 64 * half:64 * half + 64],
                             idx_k_norm_w).then_inc(vec_in, 16)

            def load(p, slot, source, guarded=True):
                if guarded:
                    sp.wait_ge(lo_ready, 2 * p - 2)
                sp.dma_start(raw[slot][:], source).then_inc(landed[slot], 16)

            def columns(first, count, source, c0):
                with sp.Fori(0, count // 2) as i:
                    for b in range(2):
                        load(2 * i + (first + b), (first + b) % 2, source[:, :, ds(512 * i + (c0 + 256 * b), 256)])

            load(0, 0, w_cols[:, :, C_IQ:C_IQ + 256], False)
            load(1, 1, w_cols[:, :, C_IQ + 256:C_IQ + 512], False)
            columns(2, 2, w_cols, C_IQ + 512)
            p = U_KI // 2
            sp.wait_ge(lo_ready, 2 * p - 2)
            for c, src, n in ((0, C_IK, 64), (64, C_IK, 64), (128, C_IW, 16)):
                sp.dma_start(raw[p % 2][:, :, c:c + n], w_cols[:, :, src:src + n]).then_inc(landed[p % 2], 16)
            columns(U_QFI // 2, 12, w_cols, C_HQ)
            columns(U_GATE // 2, 16, w_cols, C_GA)
            for b in range(2):
                load(U_ATT // 2 + b, (U_ATT // 2 + b) % 2, w_cols[:, :, C_AQ + 256 * b:C_AQ + 256 * b + 256])
            sp.wait_ge(band_zeroed, 1)
            sp.wait_ge(band_taken, 5)
            for j in range(4):
                sp.dma_start(band[32 * j:32 * j + CH, :, :].rearrange("s (a j) t -> s j a t", j=4)[:, j, :, :],
                             band_rows[:].rearrange("s (a j) t -> s j a t", j=4)[:, j, :, :])\
                    .then_inc(band_spread, 16)
            columns(U_ATT // 2 + 2, 10, w_cols, C_AQ + 512)
            columns(U_G // 2, 4, w_cols, C_HG)
            with sp.Fori(0, 4) as i:
                for b in range(2):
                    p = U_MERGE // 2 + b
                    sp.wait_ge(lo_ready, 4 * i + (2 * p - 2))
                    for branch, src in ((0, bh_cols), (1, bd_cols)):
                        sp.dma_start(raw_b[p % 2][:, branch, :, :], src[:, :, ds(512 * i + 256 * b, 256)])\
                          .then_inc(landed[p % 2], 16)
            columns(U_OUT // 2, 8, wo_cols, 0)
            for half, (u_ff, u_down) in enumerate(((U_FF, U_DOWN), (U_FF2, U_DOWN2))):
                with sp.Fori(0, FH // 2) as i:
                    for b, src in ((0, wg_cols), (1, wu_cols)):
                        load(2 * i + (u_ff // 2 + b), (u_ff // 2 + b) % 2,
                             src[:, :, ds(256 * i + half * FH * P, 256)])

                def down(p, slot, row):
                    sp.wait_ge(lo_ready, 2 * p - 2)
                    sp.dma_start(raw_d[slot], wd_rows[:, row, :]).then_inc(landed[slot], 16)

                first = u_down // 2
                down(first, first % 2, slice(half * FH, half * FH + 2))
                with sp.Fori(0, 5) as i:
                    for b in range(2):
                        down(2 * i + (first + 1 + b), (first + 1 + b) % 2, ds(4 * i + (half * FH + 2 + 2 * b), 2))
            for j in range(4):
                for t in range(2):
                    sp.wait_ge(f_copied, 2 * j + t + 1)
                    cols = slice(512 * j, 512 * j + 512)
                    sp.dma_start(out[0, P * t:P * t + P, cols], out_tok[:, t, cols]).then_inc(stored, 16)
            sp.wait_ge(stored, 8 * 16)

        @block.gpsimd
        def _(pool):
            steps = Steps(pool_step)
            for tile in (ident, bias2, onehot):
                pool.memset(tile[:], 0.0).then_inc(pool_step, 1)
            pool.memset(ones[:], 1.0).then_inc(consts, 1)
            pool.memset(keep[:], 1.0).then_inc(pool_step, 1)
            pool.memset(eps[:], EPS).then_inc(consts, 1)
            pool.wait_ge(pool_step, 4)
            steps.base = 4
            pool.affine_select(out=ident[:], in_=ident[:], compare_op=ALU.not_equal, fill=1.0, base=0,
                               pattern=[[-1, P]], channel_multiplier=1).then_inc(consts, 1)
            pool.memset(onehot[:, 15:16], 1.0).then_inc(consts, 1)
            pool.memset(keep[:].rearrange("p (c t) -> p c t", t=CH)[:, :, 0:1], 0.0).then_inc(consts, 1)
            pool.affine_select(out=bias2[:], in_=bias2[:], compare_op=ALU.is_ge, fill=-BIG, base=T0,
                               pattern=[[-1, CH]], channel_multiplier=1).then_inc(consts, 1)

            pool.wait_ge(z_free, 8 + 2)
            for j in range(2):
                pool.tensor_copy(iq_st[j][:], iq[:, j, 2:TQ]).then_inc(iq_staged, 1)
            with pool.Fori(1, 4) as i:
                for j in range(2):
                    pool.wait_ge(scored, 4 * i + (2 * j - 2))
                    pool.tensor_copy(iq_st[j][:], iq[:, ds(2 * i + j, 1), 2:TQ].rearrange("p a t -> p (a t)"))\
                        .then_inc(iq_staged, 1)
            pool.wait_ge(score_added, IDXH + 2)
            for t in range(2):
                pool.affine_select(out=score[t][:], in_=score[t][:], compare_op=ALU.is_ge, fill=FUTURE,
                                   base=META + P * t, pattern=[[-1, T]], channel_multiplier=1)\
                    .then_inc(score_masked, 1)
            for t in range(2):
                pool.wait_ge(chosen, t + 1)
                pool.affine_select(out=bias[:, t, :], in_=bias[:, t, :], compare_op=ALU.is_ge, fill=-BIG,
                                   base=META + P * t, pattern=[[-1, T]], channel_multiplier=1)\
                    .then_inc(bias_ready, 1)

            pool.memset(band[:], 0.0).then_inc(band_zeroed, 1)
            for tile in kv_st:
                pool.memset(tile[:], 0.0).then_inc(pads_zeroed, 1)
            pool.wait_ge(pads_zeroed, 2)
            pool.wait_ge(prep_done, 4)

            def stage(c, slot):
                tok = ds(c * CH, CH)
                pool.tensor_copy(kv_st[slot][:, 0, :, 0:CH], z_k[:, :, tok]).then_inc(staged, 1)
                pool.tensor_copy(kv_st[slot][:, 1, :, 0:CH], z_v[:, :, tok]).then_inc(staged, 1)
                if isinstance(c, int) and c == 0:
                    pool.wait_ge(spilled[0], 16 * 16)
                    pool.wait_ge(spilled[1], 16 * 16)
                pool.tensor_copy(q_st[slot][:], z_q[:, :, tok]).then_inc(staged, 1)
                if isinstance(c, int) and c == 0:
                    pool.wait_ge(band_spread, 64)
                pool.tensor_copy(a_st[slot][:], band[:, :, tok]).then_inc(staged, 1)

            for c in range(2):
                stage(c, c)
            with pool.Fori(1, 8) as i:
                for b in range(2):
                    pool.wait_ge(step_done, 4 * i + (2 * b - 2))
                    stage(2 * i + b, b)
            pool.wait_ge(step_done, 2 * (NC - 1) - 2)
            stage(NC - 1, (NC - 1) % 2)

            def stage_head(h):
                for n in range(3):
                    pool.tensor_copy(qkv_st[:, n, :], z_att[:, ds(h + 8 * n, 1), :].rearrange("p a t -> p (a t)"))\
                        .then_inc(qkv_staged, 1)

            pool.wait_ge(step_done, 2 * NC)
            pool.wait_ge(z_free, U_G - 32 + 2)
            stage_head(0)
            with pool.Fori(1, 8) as h:
                pool.wait_ge(logits, h)
                stage_head(h)

            def gate_pair(n, slot):
                pool.dma_start(gates[slot][:], gate_spill[:, :, :].rearrange("p (g k) t -> p g k t", g=2)
                               [:, :, n, :]).then_inc(gate_in[slot], 16)

            pool.wait_ge(qkv_staged, 3 * HEADS)
            for n in range(4):
                gate_pair(n, n)
            with pool.Fori(1, 4) as i:
                for a in range(4):
                    pool.wait_ge(m_ready, 4 * i + (a - 3))
                    pool.dma_start(gates[a][:], gate_spill[:, :, :].rearrange("p (g k) t -> p g k t", g=2)
                                   [:, :, ds(4 * i + a, 1), :].rearrange("p g k t -> p g (k t)"))\
                        .then_inc(gate_in[a], 16)

            def x_panel(slot, cols):
                pool.dma_start(x_st[slot][:, 1:3, :], x_rows[:, :, cols]).then_inc(x_st_in[slot], 16)
                pool.dma_start(x_st[slot][0:META, 0, :], meta_tokens[:, cols]).then_inc(x_st_in[slot], 16)

            def squares(n, tile, last=False):
                pool.wait_ge(out_free, n + 3)
                src = h_res[:, tile, :].rearrange("p a t -> p (a t)")
                ins = pool.tensor_tensor(h_sq[:], src, src, ALU.mult)
                if last:
                    ins.then_inc(ssq_ready, 1)
                else:
                    steps.link(pool, ins)
                    steps.link(pool, pool.tensor_tensor(ssq[:], ssq[:], h_sq[:], ALU.add))

            pool.wait_ge(o_gated, HEADS)
            steps.link(pool, pool.memset(ssq[:], 0.0))
            for b in range(2):
                x_panel(b, slice(256 * b, 256 * b + 256))
            with pool.Fori(0, 3) as i:
                steps.enter(i, 8)
                for b in range(2):
                    pool.wait_ge(xt_turned, 4 * i + (2 * b + 2))
                    x_panel(b, ds(512 * i + (512 + 256 * b), 256))
                    for a in range(2):
                        squares(4 * i + (2 * b + a), ds(4 * i + (2 * b + a), 1))
            steps.leave(3)
            for n in range(12, 16):
                if n == 15:
                    pool.tensor_copy(spare[:, 5:6], ssq[:, 0:1]).then_inc(ssq_ready, 1)
                squares(n, slice(n, n + 1), n == 15)

            pool.wait_ge(f_rs_ready, 1)
            for n, k in enumerate(range(K_POOL, KT)):
                pool.wait_ge(f_weighted, n + 1)
                pool.tensor_tensor(h_res[:, k, 2:TQ], h_res[:, k, 2:TQ], f_rs[:], ALU.mult).then_inc(f_pool_ready, 1)

        @block.tensor
        def _(pe):
            mm = nc.tensor.matmul

            def products(acc, s, ks, mov_hi, mov_lo, wk=None, first=0, last=KT - 1):
                for k in ks:
                    mm(acc, w_hi[s][:, k, :], mov_hi(k), start=(k == first), stop=False)
                    mm(acc, w_hi[s][:, k, :], mov_lo(k), start=False, stop=False)
                    ins = mm(acc, w_lo[s][:, k, :], mov_hi(k), start=False, stop=(k == last))
                return ins

            def tokens(t0, hi=u_hi, lo=u_lo, end=T):
                return lambda k: hi[:, k, t0:end], lambda k: lo[:, k, t0:end]

            def project(n, s, bank, t0, parts=((0, KT),), between=()):
                pe.wait_ge(lo_ready, n + 1)
                for q, (a, b) in enumerate(parts):
                    ins = products(ps[bank][:, 0:T - t0], s, range(a, b), *tokens(t0))
                    if q == len(parts) - 1:
                        ins.then_inc(projected, 1)
                    if q < len(between):
                        between[q]()

            pe.wait_ge(consts, 6)
            pe.wait_ge(vec_in, 16 * 12)
            for n, rows in enumerate((V_A, V_B, V_C)):
                ins = nc.tensor.transpose(ps[5 + n][:, 0:rows], vec_rows[0:rows, n, :], ident[0:rows, 0:rows])
            ins.then_inc(vec_turned, 1)
            pe.wait_ge(x_normed, 3)
            pe.wait_ge(vec_ready, 3)

            def first_units(n, ks):
                for k in ks:
                    pe.wait_ge(lo_ready, n + 1)
                    pe.wait_ge(ul_ready, k + 1)
                    ins = products(ps[n][:, 0:TQ], n, (k,), *tokens(T0))
                    if k == KT - 1:
                        ins.then_inc(projected, 1)

            beside = {9: (0, 0, 4), 10: (0, 4, 5), 11: (0, 5, 6), 12: (0, 6, 7), 13: (0, 7, 8), 14: (1, 0, 4),
                      15: (1, 4, 8)}
            for k in range(KT):
                if k >= 6:
                    pe.wait_ge(ul_ready, k - 5)
                bank, cols = ps[2 + k % 6], slice(P * k, P * k + P)
                for t in range(2):
                    nc.tensor.transpose(bank[:, META + P * t:META + P * t + P], x_tok[1 + t][:, cols], ident[:])
                nc.tensor.transpose(bank[:, 0:META], x_tok[0][0:META, cols], ident[0:META, 0:META])\
                    .then_inc(x_turned, 1)
                if k in beside:
                    n, a, b = beside[k]
                    first_units(n, range(a, b))
            for n in range(2):
                first_units(n, range(8, KT))
            for n in range(2, 8):
                pe.wait_ge(z_free, n + 1)
                project(n, n % 4, n % 2, T0)
            pe.wait_ge(z_free, 9)
            project(8, 0, 0, 0)
            pe.wait_ge(z_free, 10)
            def key_squares():
                pe.wait_ge(key_sq, 1)
                mm(ps[2][:, 0:T], ones[:], k_sq[:], start=True, stop=True).then_inc(key_sum, 1)

            project(9, 1, 1, T0, ((0, 8), (8, KT)), (key_squares,))
            pe.wait_ge(z_free, 12)
            for t in range(2):
                ins = nc.tensor.transpose(ps[6][:, 16 * t:16 * t + 16], iw_raw[0:IDXH, 2 + P * t:2 + P * t + P],
                                          ident[0:IDXH, 0:IDXH])
            ins.then_inc(iw_ready, 1)

            pe.wait_ge(key_ready, 1)
            with pe.Fori(0, 4) as i:
                for u in range(4):
                    pe.wait_ge(iq_staged, 2 * i + (u // 2 + 1))
                    pe.wait_ge(relu_done, 8 * i + (2 * u + 2))
                    half = slice(64 * (u % 2), 64 * (u % 2) + 64)
                    for t in range(2):
                        ins = mm(ps[2 + 2 * (u % 2) + t][:, 0:T], iq_st[u // 2][half, P * t:P * t + P], ki[half, :],
                                 start=True, stop=True)
                    ins.then_inc(scored, 1)
                    n = U_QFI + u
                    pe.wait_ge(z_free, 4 * i + (n + 1))
                    project(4 * i + n, n % 4, n % 2, 0)
            with pe.Fori(0, 2) as i:
                for u in range(4):
                    n = U_QFI + 16 + u
                    pe.wait_ge(z_free, 4 * i + (n + 1))
                    project(4 * i + n, n % 4, n % 2, 0)

            pe.wait_ge(z_free, U_GATE + 2)
            with pe.Fori(0, 4) as i:
                for u in range(8):
                    n = U_GATE + u
                    pe.wait_ge(gates_free, 8 * i + (u + 1))
                    project(8 * i + n, n % 4, n % 2, T0)
                    if u == 0:
                        pe.wait_ge(band_taken, i + 1)
                    for s in (2 * u, 2 * u + 1):
                        pe.wait_ge(pair_ready, 16 * i + (s + 1))
                        for a in range(2):
                            o = ps[2 + a][0:CH, 0:T].rearrange("p (c t) -> p c t", t=CH)[:, :, s:CH]
                            r = pairs[s % 2][:, NC * a:NC * a + NC, s:CH]
                            ins = mm(o, onehot[:, 15 - s:31 - s], r, start=(s == 0), stop=(s == CH - 1))
                        ins.then_inc(band_used, 1)

            def turn(slot, h0, st, col=0):
                pe.wait_ge(staged, st - 2)
                pe.wait_ge(band_taken, 5)
                for n in range(2):
                    ins = nc.tensor.transpose(ps[2][:, P * (n + col):P * (n + col) + P],
                                              kv_st[slot][:, n, h0:h0 + 4, :].rearrange("p h t -> p (h t)"), ident[:])
                ins.then_inc(turned, 1)

            def step(k, slot, h0, st, update=True, kv_tok=kv_tok, o_bank=5):
                pe.wait_ge(staged, st)
                pe.wait_ge(tok_copied, k + 1)
                pe.wait_ge(state_ready, min(k, 32) + 2 if isinstance(k, int) else k + 2)
                o = ps[o_bank][:, 0:4 * CH]
                mm(o, kv_tok[:, 1, :], a_st[slot][:, h0:h0 + 4, :].rearrange("p h t -> p (h t)"),
                   start=True, stop=False, skip_group_check=True)
                for j in range(4):
                    ins = mm(o[:, CH * j:CH * j + CH], state[:, h0 + j, :], q_st[slot][:, h0 + j, :],
                             start=False, stop=True, skip_group_check=True)
                if update:
                    for j in range(4):
                        tok = slice(32 * j, 32 * j + CH)
                        ins = mm(ps[UPDATE_BANKS[j]][:, 0:P], kv_tok[tok, 0, :], kv_tok[tok, 1, :],
                                 start=True, stop=True)
                ins.then_inc(step_done, 1)

            def half_chunk(i, k):
                c = k // 2
                return 16 * i + k, c % 2, 4 * (k % 2), 32 * i + 4 * (c + 1)

            when = ([(8, 12)], [(5, 9)], [(1, 4), (12, 16)])
            pe.wait_ge(gates_free, 32 + 2)
            with pe.Fori(0, 2) as i:
                for u in range(12):
                    n = U_ATT + u
                    pe.wait_ge(z_free, 12 * i + (n - 32 + 1))
                    cuts, jobs = [0], []
                    for j, (t_turn, t_step) in enumerate(when[u % 3]):
                        kk, slot, h0, st = half_chunk(i, 4 * (u // 3) + u % 3 + j)
                        cuts += [t_turn, t_step]
                        jobs += [lambda a=(slot, h0, st): turn(*a), lambda a=(kk, slot, h0, st): step(*a)]
                    if cuts[-1] < KT:
                        cuts.append(KT)
                    project(12 * i + n, n % 4, n % 2, 0, tuple(zip(cuts, cuts[1:])), jobs)
            turn(0, 0, 4 * NC)
            turn(0, 4, 4 * NC, 2)
            step(32, 0, 0, 4 * NC, False)
            step(33, 0, 4, 4 * NC, False, kv_tok2, 3)

            pe.wait_ge(o_sq_ready, 2)
            for h in range(HEADS):
                if h >= 6:
                    pe.wait_ge(o_std, h - 5)
                mm(ps[2 + h % 6][:, 0:TQ], ones[:], o_sq[:, h, :], start=True, stop=True).then_inc(o_sum, 1)
            pe.wait_ge(o_std, HEADS)

            with pe.Fori(0, 2) as i:
                for u in range(4):
                    pe.wait_ge(qkv_staged, 12 * i + 3 * (u + 1))
                    for m, (a, b) in enumerate(((0, META), (META, META + P), (META + P, T))):
                        ins = nc.tensor.transpose(ps[6][0:b - a, P * m:P * m + P], qkv_st[:, 2, a:b], ident[:])
                    ins.then_inc(v_turned, 1)
                    for t in range(2):
                        mm(ps[4 + t][:, 0:T], qkv_st[:, 0, META + P * t:META + P * t + P], qkv_st[:, 1, :],
                           start=True, stop=True)
                    mm(ps[4][0:2, T:T + CH], qkv_st[:, 0, T0:META], qkv_st[:, 1, 0:CH],
                       start=True, stop=True).then_inc(logits, 1)

                    def turn_p(i=i, u=u):
                        pe.wait_ge(p_ready, 4 * i + (u + 1))
                        pe.wait_ge(v_copied, 8 * i + 2 * (u + 1))
                        for t in range(2):
                            nc.tensor.transpose(ps[7][0:CH, 2 + P * t:2 + P * t + P], probs[:, t, 0:META], ident[:])
                            for m in range(2):
                                nc.tensor.transpose(ps[6][:, SEQ * m + P * t:SEQ * m + P * t + P],
                                                    probs[:, t, META + P * m:META + P * m + P], ident[:])
                        nc.tensor.transpose(ps[7][0:CH, 0:2], probs2[:], ident[0:2, 0:2]).then_inc(p_turned, 1)

                    def values(i=i, u=u):
                        pe.wait_ge(p_copied, 8 * i + 2 * (u + 1))
                        pe.wait_ge(ya_ready, 4 * i + (u + 1))
                        mm(ps[2][:, 0:TQ], v_keys[0:CH, 0, :], p_meta[:], start=True, stop=False)
                        mm(ps[2][:, 2:TQ], v_keys[:, 1, :], p_keys[:, 0, :], start=False, stop=False)
                        mm(ps[2][:, 2:TQ], v_keys[:, 2, :], p_keys[:, 1, :], start=False, stop=True)\
                            .then_inc(pv_done, 1)

                    n = U_G + u
                    pe.wait_ge(z_free, 4 * i + (n - 32 + 1))
                    project(4 * i + n, n % 4, n % 2, T0, ((0, 13), (13, KT)), (turn_p, values))

            def attention_part(n, u):
                products(ps[2 * (u % 2) + 1][:, 0:TQ], n % 4, range(8, 15), lambda k: ya_hi[:, k - 8, :],
                         lambda k: ya_lo[:, k - 8, :], first=8)
                if n == U_MERGE:
                    pe.wait_ge(ya_ready, 9)
                products(ps[2 * (u % 2) + 1][:, 0:TQ], n % 4, (15,), lambda k: ya_hi[:, k - 8, :],
                         lambda k: ya_lo[:, k - 8, :], first=8)

            def hgrn_part(n, u):
                for k in range(8):
                    if n == U_MERGE:
                        pe.wait_ge(yh_ready, k + 1)
                    ins = products(ps[2 * (u % 2)][:, 0:TQ], n % 4, (k,), lambda k: yh_hi[:, k, :],
                                   lambda k: yh_lo[:, k, :], last=7)
                ins.then_inc(projected, 1)

            pe.wait_ge(z_free, U_MERGE - 32 + 2)
            pe.wait_ge(ya_ready, 8)
            pe.wait_ge(lo_ready, U_MERGE + 1)
            attention_part(U_MERGE, 0)
            pe.wait_ge(lo_ready, U_MERGE + 2)
            attention_part(U_MERGE + 1, 1)
            hgrn_part(U_MERGE, 0)
            hgrn_part(U_MERGE + 1, 1)
            for n in (U_MERGE + 2, U_MERGE + 3):
                pe.wait_ge(lo_ready, n + 1)
                pe.wait_ge(merge_free, n - U_MERGE + 1)
                attention_part(n, n - U_MERGE)
                hgrn_part(n, n - U_MERGE)
            with pe.Fori(0, 3) as i:
                for u in range(4):
                    n = U_MERGE + 4 + u
                    pe.wait_ge(lo_ready, 4 * i + (n + 1))
                    pe.wait_ge(merge_free, 4 * i + (u + 5))
                    attention_part(n, u)
                    hgrn_part(n, u)

            pe.wait_ge(merge_free, 17)
            pe.wait_ge(m_ready, 14)
            with pe.Fori(0, 4) as i:
                for u in range(4):
                    n = U_OUT + u
                    if u % 2 == 0:
                        pe.wait_ge(x_st_in[u // 2], 32 * i + 32)
                    pe.wait_ge(out_free, 4 * i + (u + 1))
                    bank = 4 + u % 2
                    for t in range(2):
                        nc.tensor.transpose(ps[bank][:, META + P * t:META + P * t + P],
                                            x_st[u // 2][:, 1 + t, P * (u % 2):P * (u % 2) + P], ident[:])
                    nc.tensor.transpose(ps[bank][:, 0:META], x_st[u // 2][0:META, 0, P * (u % 2):P * (u % 2) + P],
                                        ident[0:META, 0:META]).then_inc(xt_turned, 1)
                    pe.wait_ge(lo_ready, 4 * i + (n + 1))
                    for k in range(KT):
                        if u == 0 and k >= 14:
                            pe.wait_ge(m_ready, k + 1)
                        ins = products(ps[u % 2][:, 0:TQ], n % 4, (k,), lambda k: m_hi[:, k, :], lambda k: m_lo[:, k, :])
                    ins.then_inc(projected, 1)
            pe.wait_ge(ssq_ready, 1)
            mm(ps[6][:, 0:TQ], ones[:], ssq[:], start=True, stop=False)
            pe.wait_ge(ssq_ready, 2)
            mm(ps[6][:, 0:TQ], ones[:], h_sq[:], start=False, stop=True).then_inc(ssq_sum, 1)

            for half, (u_ff, u_down) in enumerate(((U_FF, U_DOWN), (U_FF2, U_DOWN2))):
                def gate_up(u, ks, half=half, u_ff=u_ff):
                    t0, cols = (0, TQ) if u < 2 else (2, SEQ)
                    ins = products(ps[4 * half + u][:, 0:cols], (u_ff + u) % 4, ks, *tokens(t0, m_hi, m_lo, TQ))
                    if ks[-1] == KT - 1:
                        ins.then_inc(projected, 1)

                if half == 0:
                    pe.wait_ge(out_free, 18)
                    pe.wait_ge(lo_ready, u_ff + 3)
                    for k in range(KT):
                        pe.wait_ge(u2l_ready, k + 1)
                        for u in range(3):
                            gate_up(u, (k,))
                    pe.wait_ge(lo_ready, u_ff + 4)
                    gate_up(3, range(KT))
                else:
                    pe.wait_ge(down_added, 4)
                with pe.Fori(1 - half, FH // 2) as i:
                    for u in range(4):
                        pe.wait_ge(lo_ready, 4 * i + (u_ff + u + 1))
                        pe.wait_ge(ff_taken, 4 * i + (2 * FH * half + u + 1))
                        gate_up(u, range(KT))

                def down(n, s, u, tile, half=half):
                    pe.wait_ge(lo_ready, n + 1)
                    first = isinstance(tile, int) and tile == 0
                    for kk in range(2):
                        t = tile + kk
                        mh, ml = ((hid_hi[:, t, :], hid_lo[:, t, :]) if first else
                                  (hid_hi[:, ds(t, 1), :].rearrange("p a t -> p (a t)"),
                                   hid_lo[:, ds(t, 1), :].rearrange("p a t -> p (a t)")))
                        for g in range(8):
                            acc = ps[4 * ((u + half + 1) % 2) + g // 2][:, SEQ * (g % 2):SEQ * (g % 2) + SEQ]
                            w = 8 * kk + g
                            mm(acc, w_hi[s][:, w, :], mh, start=(first and kk == 0 and g % 2 == 0), stop=False,
                               skip_group_check=True)
                            mm(acc, w_hi[s][:, w, :], ml, start=False, stop=False, skip_group_check=True)
                            ins = mm(acc, w_lo[s][:, w, :], mh, start=False, stop=True, skip_group_check=True)
                    ins.then_inc(projected, 1)

                if half == 1:
                    pe.wait_ge(down_added, 8)
                pe.wait_ge(hidl_ready, FH * half + 2)
                down(u_down, u_down % 4, 0, 0)
                pe.wait_ge(ff_taken, 2 * FH * (half + 1) + 4)
                down(u_down + 1, (u_down + 1) % 4, 1, 0)
                pe.wait_ge(hidl_ready, FH * (half + 1))
                with pe.Fori(0, 5) as i:
                    for u in range(4):
                        n = u_down + 2 + u
                        down(4 * i + n, n % 4, u % 2, 4 * i + (2 + 2 * (u // 2)))

            pe.wait_ge(f_half, 1)
            mm(ps[0][:, 0:SEQ], ones[:], f_sq[0][:, 0, :], start=True, stop=False)
            for b in range(4, 8):
                pe.wait_ge(f_sq_ready, b + 1)
                for a in range(2):
                    ins = mm(ps[0][:, 0:SEQ], ones[:], f_sq[b][:, a, :], start=False, stop=(b + a == 8))
            ins.then_inc(f_sum, 1)
            for j in range(4):
                pe.wait_ge(f_ready, min(4 * (j + 1), K_POOL))
                if 4 * (j + 1) > K_POOL:
                    pe.wait_ge(f_pool_ready, 4 * (j + 1) - K_POOL)
                for t in range(2):
                    for k in range(4 * j, 4 * j + 4):
                        ins = nc.tensor.transpose(ps[2 * j + t][:, P * (k % 4):P * (k % 4) + P],
                                                  h_res[:, k, 2 + P * t:2 + P * t + P], ident[:])
                    ins.then_inc(f_turned, 1)

        @block.scalar
        def _(act):
            activation = nc.scalar.activation

            def settle():
                act.wait_ge(consts, 6)

            def round_unit(n, m, landed_at):
                if m > 3:
                    act.wait_ge(projected, n - 3)
                if m % 2 == 0:
                    act.wait_ge(landed[(m // 2) % 2], landed_at)
                activation(w_hi[m % 4][:], raw[(m // 2) % 2][:, :, P * (m % 2):P * (m % 2) + P], ACT.Copy)\
                    .then_inc(hi_ready, 1)

            def ahead(n):
                if n + 3 < U_END:
                    round_unit(n + 3, n + 3, landed_by[(n + 3) // 2])

            def pace(n0, per, times):
                out = []
                for u in range(per):
                    units = [n0 + 3 + u + per * t for t in range(times)]
                    if units[-1] >= U_END:
                        return None
                    at = [landed_by[m // 2] for m in units]
                    grows = {b - a for a, b in zip(at, at[1:])}
                    if len(grows) > 1:
                        return None
                    out.append(grows.pop())
                return out

            def loop(n0, per, times, body, early=0):
                full = times
                while full > 1 and pace(n0 + early, per, full) is None:
                    full -= 1
                if full > 1:
                    grows = pace(n0 + early, per, full)
                    with act.Fori(0, full) as i:
                        for u in range(per):
                            m = n0 + early + u + 3
                            body(i, u, lambda m=m, g=grows[u]: round_unit(per * i + m, m, g * i + landed_by[m // 2]))
                for i in range(full if full > 1 else 0, times):
                    for u in range(per):
                        body(i, u, lambda n=n0 + early + per * i + u: ahead(n))

            act.wait_ge(consts, 6)
            activation(spare[:, 0:1], eps[:], ACT.Sqrt).then_inc(gates_free, 2)
            activation(spare[:, 1:2], eps[:], ACT.Copy).then_inc(relu_done, 4)
            act.wait_ge(z_free, 2)
            for t, rows in enumerate((META, P, P)):
                act.wait_ge(x_in[t], 16)
                activation(junk[0:rows, :], x_tok[t][0:rows, :], ACT.Square,
                           accum_out=rstat[0:rows, t:t + 1]).then_inc(x_sum, 1)
                act.wait_ge(x_sum, t + 1)
            activation(rstat[:, 3:6], rstat[:, 0:3], ACT.Sqrt, bias=eps[:], scale=1.0 / D).then_inc(x_std, 1)
            act.wait_ge(x_rstd, 1)
            activation(x_tok[2][:], x_tok[2][:], ACT.Copy, scale=rstat[:, 2:3]).then_inc(x_normed, 1)
            act.wait_ge(vec_ready, 3)
            for k in range(KT):
                if k in (4, 8):
                    round_unit(k // 4 - 1, k // 4 - 1, landed_by[0])
                act.wait_ge(x_turned, k + 1)
                activation(u_hi[:, k, :], ps[2 + k % 6][:, 0:T], ACT.Copy, scale=vec_a[:, V_ATTN + k:V_ATTN + k + 1])\
                    .then_inc(uh_ready, 1)
            round_unit(2, 2, landed_by[1])
            act.wait_ge(lb_diff, 1)
            activation(lb[:, 1:3, :], lb[:, 1:3, :], ACT.Exp).then_inc(lb_exp, 1)

            for n in range(9):
                ahead(n)
            act.wait_ge(z_free, 8 + 1 + 2)
            activation(k_sq[:], k_raw[:], ACT.Square).then_inc(key_sq, 1)
            act.wait_ge(key_sum, 1)
            activation(k_rs[:], ps[2][:, 0:T], ACT.Sqrt, bias=eps[:], scale=1.0 / P).then_inc(key_std, 1)
            ahead(9)

            def score_unit(i, u, split):
                act.wait_ge(scored, 4 * i + (u + 1))
                act.wait_ge(score_added, 4 * i + (u + 1))
                for t in range(2):
                    activation(relu[u % 2][t][:], ps[2 + 2 * (u % 2) + t][:, 0:T], ACT.Relu).then_inc(relu_done, 1)
                split()

            loop(U_QFI, 4, 4, score_unit)
            for u in range(8):
                n = U_QFI + 16 + u
                ahead(n)
                if u == 1:
                    act.wait_ge(z_free, U_QFI + 16 + 2)
                    activation(sig[:], z_k[:], ACT.Sigmoid).then_inc(sig_ready, 1)
                    act.wait_ge(sig_ready, 1)
                    activation(z_k[:], z_k[:], ACT.Sigmoid, scale=-1.0).then_inc(sig_ready, 1)
                if u == 2:
                    activation(z_q[:], z_q[:], ACT.Silu).then_inc(sig_ready, 1)
                if u == 5:
                    act.wait_ge(forget_ready, 1)
                    activation(z_b[:], sig[:], ACT.Ln).then_inc(log_ready, 1)

            def decays(i, u):
                for s in (2 * u, 2 * u + 1):
                    act.wait_ge(diff_ready, 16 * i + (s + 1))
                    activation(diff[s % 2][:, :, s:CH], diff[s % 2][:, :, s:CH], ACT.Exp).then_inc(decay_ready, 1)

            def gate_unit(i, u, split):
                if u == 0:
                    decays(i, 0)
                split()
                if u < 7:
                    decays(i, u + 1)
                else:
                    act.wait_ge(pair_ready, 16 * i + 16)
                    settle()
                    zb = z_b[:].rearrange("p h t -> p (h t)")[:, ds(2 * T * i, 2 * T)]
                    activation(diff[0][:].rearrange("p c t -> p (c t)"), zb, ACT.Exp).then_inc(prep_e, 1)
                    act.wait_ge(prep_d, i + 1)
                    dec = decay[:].rearrange("p h c -> p (h c)")[:, ds(2 * NC * i, 2 * NC)]
                    activation(dec, dec, ACT.Exp).then_inc(prep_x, 1)
                    activation(diff[1][:].rearrange("p c t -> p (c t)"), zb, ACT.Exp).then_inc(prep_x, 1)
                b = u % 2
                if u >= 2:
                    act.wait_ge(spilled[b], 64 * i + 16 * (u // 2))
                act.wait_ge(projected, 8 * i + (U_GATE + u + 1))
                activation(gate_st[b][:], ps[(U_GATE + u) % 2][:, 0:TQ], ACT.Copy).then_inc(gates_free, 1)
                act.wait_ge(gates_free, 8 * i + (u + 3))
                act.dma_start(gate_spill[:, ds(8 * i + u, 1), :].rearrange("p a t -> p (a t)"), gate_st[b][:])\
                    .then_inc(spilled[b], 16)
                if u == 7:
                    for q in range(2):
                        act.wait_ge(spilled[q], 64 * i + 64)

            loop(U_GATE, 8, 4, gate_unit)
            def copy_tok(k):
                act.wait_ge(turned, k + 1)
                activation(kv_tok[:].rearrange("p a b -> p (a b)"), ps[2][:, 0:2 * P], ACT.Copy).then_inc(tok_copied, 1)

            def att_unit(i, u, split):
                k = 4 * (u // 3) + u % 3
                if u % 3 == 2:
                    copy_tok(16 * i + k)
                    split()
                    copy_tok(16 * i + (k + 1))
                else:
                    split()
                    copy_tok(16 * i + k)

            loop(U_ATT, 12, 2, att_unit)
            edge = T - CH
            act.wait_ge(turned, 34)
            copy_tok(32)
            activation(kv_tok2[:].rearrange("p a b -> p (a b)"), ps[2][:, 2 * P:4 * P], ACT.Copy)\
                .then_inc(tok_copied, 1)
            act.wait_ge(staged, 4 * NC)
            act.wait_ge(state_ready, 2 * (NC - 1) + 2)
            activation(o_sq[:, :, 0:edge - T0], z_v[:, :, T0:edge], ACT.Square).then_inc(o_sq_ready, 1)
            act.wait_ge(state_ready, 2 * NC + 2)
            activation(o_sq[:, :, edge - T0:TQ], z_v[:, :, edge:T], ACT.Square).then_inc(o_sq_ready, 1)
            for h in range(HEADS):
                act.wait_ge(o_sum, h + 1)
                activation(o_rs[:, h, :], ps[2 + h % 6][:, 0:TQ], ACT.Sqrt, bias=eps[:], scale=1.0 / P)\
                    .then_inc(o_std, 1)

            def head_unit(i, u, split):
                h1 = 4 * i + (u + 1)
                act.wait_ge(v_turned, h1)
                activation(v_keys[0:CH, 0, :], ps[6][0:CH, 0:P], ACT.Copy).then_inc(v_copied, 1)
                activation(v_keys[:, 1:3, :], ps[6][:, P:3 * P].rearrange("p (a b) -> p a b", a=2), ACT.Copy)\
                    .then_inc(v_copied, 1)
                act.wait_ge(max_ready, h1)
                for t in range(2):
                    activation(probs[:, t, :], probs[:, t, :], ACT.Exp, bias=stat[:, t:t + 1],
                               accum_out=stat[:, 4 + t:5 + t]).then_inc(exp_done, 1)
                activation(probs2[:], probs2[:], ACT.Exp, bias=stat[0:2, 2:3], accum_out=stat[0:2, 6:7])\
                    .then_inc(exp_done, 1)
                split()
                act.wait_ge(p_turned, h1)
                activation(p_keys[:].rearrange("p a b -> p (a b)"), ps[6][:], ACT.Copy).then_inc(p_copied, 1)
                activation(p_meta[:], ps[7][0:CH, 0:TQ], ACT.Copy).then_inc(p_copied, 1)
                act.wait_ge(pv_done, h1)
                settle()
                activation(ya_hi[:, ds(4 * i + u, 1), :].rearrange("p a t -> p (a t)"), ps[2][:, 0:TQ], ACT.Copy)\
                    .then_inc(ya_hi_ready, 1)

            loop(U_G, 4, 2, head_unit)

            act.wait_ge(z_free, U_MERGE - 32 + 2)
            for h in range(HEADS + 1):
                if h < HEADS:
                    activation(z_g[:, h, :], z_g[:, h, :], ACT.Silu).then_inc(g_ready, 1)
                if h:
                    act.wait_ge(o_gated, h)
                    activation(yh_hi[:, h - 1, :], z_v[:, h - 1, T0:T], ACT.Copy).then_inc(yh_hi_ready, 1)

            def merge_unit(i, u, split):
                act.wait_ge(gate_in[u], 16 * i + 16)
                activation(gates[u][:], gates[u][:], ACT.Sigmoid).then_inc(gate_sig, 1)
                split()
                act.wait_ge(m_sum, 4 * i + (u + 1))
                settle()
                activation(m_hi[:, ds(4 * i + u, 1), :].rearrange("p a t -> p (a t)"), gates[u][:, 0, :], ACT.Copy)\
                    .then_inc(mh_ready, 1)

            ahead(U_MERGE)
            loop(U_MERGE, 4, 4, merge_unit, early=1)

            def out_unit(i, u, split):
                act.wait_ge(xt_turned, 4 * i + (u + 1))
                settle()
                activation(h_res[:, ds(4 * i + u, 1), :].rearrange("p a t -> p (a t)"), ps[4 + u % 2][:, T0:T],
                           ACT.Copy).then_inc(xt_ready, 1)
                split()

            loop(U_OUT, 4, 4, out_unit, early=1)
            act.wait_ge(ssq_sum, 1)
            activation(h_rs[:], ps[6][:, 0:TQ], ACT.Sqrt, bias=eps[:], scale=1.0 / D).then_inc(h_std, 1)
            for k in range(KT):
                act.wait_ge(u2_ready, k + 1)
                activation(m_hi[:, k, :], u_tmp[k % 4][:], ACT.Copy).then_inc(u2h_ready, 1)

            for half, (u_ff, u_down) in enumerate(((U_FF, U_DOWN), (U_FF2, U_DOWN2))):
                def ff_unit(i, u, split, half=half):
                    split()
                    if u < 2:
                        act.wait_ge(ff_taken, 4 * i + (2 * FH * half + u + 5))
                        activation(conv[u][:], conv[u][:], ACT.Silu).then_inc(silu_ready, 1)
                    else:
                        a = u - 2
                        act.wait_ge(ff_taken, 4 * i + (2 * FH * half + u + 5))
                        settle()
                        activation(hid_hi[:, ds(2 * i + a, 1), :].rearrange("p a t -> p (a t)"), conv[a][:], ACT.Copy)\
                            .then_inc(hidh_ready, 1)

                if half == 1:
                    ahead(u_ff)
                loop(u_ff, 4, FH // 2, ff_unit, early=1)
                ahead(u_down + 1)
                loop(u_down + 2, 4, 5, lambda i, u, split: split())

            for b in range(8):
                act.wait_ge(down_added, 8 + b + 1)
                act_in = h_res[:].rearrange("p (g u) t -> p u g t", u=2)[:, b // 4, 2 * (b % 4):2 * (b % 4) + 2, 2:TQ]
                activation(f_sq[b][:], act_in, ACT.Square).then_inc(f_sq_ready, 1)
            act.wait_ge(f_sum, 1)
            activation(f_rs[:], ps[0][:, 0:SEQ], ACT.Sqrt, bias=eps[:], scale=1.0 / D).then_inc(f_std, 1)
            act.wait_ge(f_sq_ready, 8)
            for k in range(K_POOL, KT):
                activation(h_res[:, k, 2:TQ], h_res[:, k, 2:TQ], ACT.Copy, scale=vec_c[:, V_FIN + k:V_FIN + k + 1])\
                    .then_inc(f_weighted, 1)
            for j in range(4):
                for t in range(2):
                    act.wait_ge(f_turned, 2 * j + t + 1)
                    activation(out_tok[:, t, 512 * j:512 * j + 512], ps[2 * j + t][:], ACT.Copy).then_inc(f_copied, 1)

        @block.vector
        def _(dve):
            v = nc.vector
            steps = Steps(dve_step)
            link = lambda ins: steps.link(dve, ins)

            def rest(n, m):
                dve.wait_ge(hi_ready, n + 1)
                v.tensor_tensor(w_lo[m % 4][:], raw[(m // 2) % 2][:, :, P * (m % 2):P * (m % 2) + P],
                                w_hi[m % 4][:].bitcast(F32), ALU.subtract).then_inc(lo_ready, 1)

            def ahead(n, m):
                if isinstance(n, int) and n + 3 >= U_END:
                    return
                rest(n + 3, m + 3)

            v.memset(rstat[:], 1.0).then_inc(z_free, 2)
            v.memset(lb[:], 0.0).then_inc(ff_taken, 4)
            v.memset(spare[:, 2:3], 0.0).then_inc(merge_free, 2)
            v.memset(spare[:, 3:4], 0.0).then_inc(out_free, 2)
            v.memset(spare[:, 4:5], 0.0).then_inc(band_taken, 1)
            dve.wait_ge(vec_turned, 1)
            for n, (dst, cols) in enumerate(((vec_a, V_A), (vec_b, V_B), (vec_c, V_C))):
                v.tensor_copy(dst[:], ps[5 + n][:, 0:cols]).then_inc(vec_ready, 1)
            dve.wait_ge(x_sum, 3)
            dve.wait_ge(x_std, 1)
            v.reciprocal(rstat[:, 0:3], rstat[:, 3:6]).then_inc(x_rstd, 1)
            dve.wait_ge(x_rstd, 1)
            for t, rows in ((1, P), (0, META)):
                v.tensor_scalar(x_tok[t][0:rows, :], x_tok[t][0:rows, :], rstat[0:rows, t:t + 1], None, ALU.mult)\
                    .then_inc(x_normed, 1)
            dve.wait_ge(vec_ready, 3)
            link(v.tensor_tensor(lb[:, 0, :], vec_a[:, V_LB0:V_LB0 + 8], vec_a[:, V_LB1:V_LB1 + 8], ALU.max))
            v.tensor_tensor(lb[:, 1, :], vec_a[:, V_LB0:V_LB0 + 8], lb[:, 0, :], ALU.subtract)
            v.tensor_tensor(lb[:, 2, :], vec_a[:, V_LB1:V_LB1 + 8], lb[:, 0, :], ALU.subtract).then_inc(lb_diff, 1)
            for k in range(KT):
                if k in (4, 8):
                    rest(k // 4 - 1, k // 4 - 1)
                dve.wait_ge(uh_ready, k + 1)
                v.scalar_tensor_tensor(u_lo[:, k, :], ps[2 + k % 6][:, 0:T], vec_a[:, V_ATTN + k:V_ATTN + k + 1],
                                       u_hi[:, k, :].bitcast(F32), ALU.mult, ALU.subtract).then_inc(ul_ready, 1)
            rest(2, 2)
            dve.wait_ge(lb_exp, 1)
            link(v.tensor_tensor(lb[:, 0, :], lb[:, 1, :], lb[:, 2, :], ALU.add))
            link(v.reciprocal(lb[:, 0, :], lb[:, 0, :]))
            v.tensor_tensor(lb[:, 3, :], lb[:, 2, :], lb[:, 0, :], ALU.mult)
            link(v.tensor_tensor(lb[:, 1, :], lb[:, 1, :], lb[:, 0, :], ALU.mult))

            with dve.Fori(0, 2) as i:
                for u in range(4):
                    ahead(4 * i + u, u)
                    dve.wait_ge(projected, 4 * i + (u + 1))
                    v.tensor_copy(iq[:, ds(4 * i + u, 1), :].rearrange("p a t -> p (a t)"), ps[u % 2][:, 0:TQ])\
                        .then_inc(z_free, 1)
            dve.wait_ge(projected, 9)
            v.tensor_copy(k_raw[:], ps[0][:, 0:T]).then_inc(z_free, 1)
            ahead(8, 8)
            dve.wait_ge(key_std, 1)
            link(v.reciprocal(k_rs[:], k_rs[:]))
            v.scalar_tensor_tensor(ki[:], k_raw[:], vec_a[:, V_IDXK:V_IDXK + 1], k_rs[:], ALU.mult, ALU.mult)\
                .then_inc(key_ready, 1)
            v.memset(score[0][:], 0.0)
            v.memset(score[1][:], 0.0).then_inc(score_added, 2)
            dve.wait_ge(projected, 10)
            v.tensor_copy(iw_raw[0:IDXH, :], ps[1][0:IDXH, 0:TQ]).then_inc(z_free, 1)
            dve.wait_ge(iw_ready, 1)
            v.tensor_scalar(iw_tok[:].rearrange("p a b -> p (a b)"), ps[6][:, 0:32],
                            (IDXH ** -0.5) * (64 ** -0.5), None, ALU.mult).then_inc(key_ready, 1)
            ahead(9, 9)
            dve.wait_ge(key_ready, 2)

            with dve.Fori(0, 4) as i:
                for u in range(4):
                    m = U_QFI + u
                    dve.wait_ge(relu_done, 8 * i + (2 * u + 2 + 4))
                    dve.wait_ge(score_added, 4 * i + (u + 2))
                    for t in range(2):
                        ins = v.scalar_tensor_tensor(score[t][:], relu[u % 2][t][:],
                                                     iw_tok[:, t, ds(4 * i + u, 1)], score[t][:], ALU.mult, ALU.add)
                    ins.then_inc(score_added, 1)
                    ahead(4 * i + m, m)
                    dve.wait_ge(projected, 4 * i + (m + 1))
                    v.tensor_copy(z_qf[:, ds(4 * i + u, 1), :].rearrange("p a t -> p (a t)"), ps[m % 2][:, 0:T])\
                        .then_inc(z_free, 1)

            def top_keys(t, rounds):
                for r in range(rounds):
                    link(v.max(top8[:], score[t][:]))
                    link(v.match_replace(score[t][:], top8[:], score[t][:], TAKEN))

            for u in range(8):
                m = U_QFI + 16 + u
                if u == 0:
                    dve.wait_ge(score_masked, 2)
                if u < 4:
                    top_keys(u // 2, 4)
                    if u % 2:
                        t = u // 2
                        link(v.tensor_scalar(bias[:, t, :], score[t][:], TAKEN, BIG, ALU.is_equal, ALU.mult))
                        v.tensor_scalar(bias[:, t, :], bias[:, t, :], -BIG, None, ALU.add).then_inc(chosen, 1)
                if u == 4:
                    dve.wait_ge(sig_ready, 2)
                    for h in range(HEADS):
                        v.tensor_scalar(z_k[:, h, :], z_k[:, h, :], lb[:, 3, h:h + 1], None, ALU.mult)
                        ins = v.tensor_scalar(sig[:, h, :], sig[:, h, :], lb[:, 3, h:h + 1], lb[:, 1, h:h + 1],
                                              ALU.mult, ALU.add)
                    ins.then_inc(forget_ready, 1)
                if u == 6:
                    dve.wait_ge(log_ready, 1)
                    for h in range(HEADS):
                        ins = v.tensor_tensor_scan(z_b[:, h, :], keep[:], z_b[:, h, :], 0.0, ALU.mult, ALU.add)
                    link(ins)
                ahead(m, m)
                dve.wait_ge(projected, m + 1)
                v.tensor_copy(z_v[:, u, :], ps[m % 2][:, 0:T]).then_inc(z_free, 1)

            zf = lambda z, i: z[:].rearrange("p h t -> p (h t)")[:, ds(2 * T * i, 2 * T)]\
                .rearrange("p (c t) -> p c t", t=CH)

            def differences(i, u):
                for s in (2 * u, 2 * u + 1):
                    v.tensor_tensor(diff[s % 2][:, :, s:CH], zf(z_b, i)[:, :, s:CH],
                                    zf(z_b, i)[:, :, s:s + 1].to_broadcast([P, 2 * NC, CH - s]), ALU.subtract)\
                        .then_inc(diff_ready, 1)

            dve.wait_ge(sig_ready, 3)
            with dve.Fori(0, 4) as i:
                steps.enter(i, 17)
                for u in range(8):
                    m = U_GATE + u
                    if u == 0:
                        differences(i, 0)
                    for s in (2 * u, 2 * u + 1):
                        w = CH - s
                        dve.wait_ge(decay_ready, 16 * i + (s + 1))
                        link(v.tensor_tensor(diff[s % 2][:, :, s:CH], diff[s % 2][:, :, s:CH],
                                             zf(z_k, i)[:, :, s:s + 1].to_broadcast([P, 2 * NC, w]), ALU.mult))
                        if s >= 2:
                            dve.wait_ge(band_used, 16 * i + (s - 1))
                        v.tensor_tensor(pairs[s % 2][:, :, s:CH], diff[s % 2][:, :, s:CH],
                                        zf(z_q, i)[:, :, s:CH], ALU.mult).then_inc(pair_ready, 1)
                    if u < 7:
                        dve.wait_ge(pair_ready, 16 * i + 2 * (u + 1))
                        differences(i, u + 1)
                    ahead(8 * i + m, m)
                dec = decay[:].rearrange("p h c -> p (h c)")[:, ds(2 * NC * i, 2 * NC)]\
                    .rearrange("p (c a) -> p c a", a=1)
                link(v.tensor_copy(dec, zf(z_b, i)[:, :, CH - 1:CH]))
                dve.wait_ge(prep_e, i + 1)
                v.tensor_tensor(zf(z_b, i), dec.to_broadcast([P, 2 * NC, CH]), zf(z_b, i), ALU.subtract)\
                    .then_inc(prep_d, 1)
                v.tensor_tensor(zf(z_q, i), zf(z_q, i), diff[0][:], ALU.mult)
                dve.wait_ge(prep_x, 2 * i + 2)
                v.tensor_tensor(zf(z_k, i), zf(z_k, i), diff[1][:], ALU.mult).then_inc(prep_done, 1)
                dve.wait_ge(prep_done, i + 1)
                dve.wait_ge(band_used, 16 * i + 16)
                for a in range(2):
                    ins = v.tensor_copy(band_rows[:, ds(2 * i + a, 1), :].rearrange("p a t -> p (a t)"),
                                        ps[2 + a][0:CH, 0:T])
                ins.then_inc(band_taken, 1)
            steps.leave(4)

            v.memset(state[:], 0.0).then_inc(state_ready, 2)

            def advance(k, c, h0, update=True, o_bank=5):
                dve.wait_ge(step_done, k + 1)
                o = v.tensor_copy(z_v[:, h0:h0 + 4, ds(c * CH, CH)],
                                  ps[o_bank][:, 0:4 * CH].rearrange("p (h t) -> p h t", h=4))
                if not update:
                    o.then_inc(state_ready, 1)
                    return
                s = state[:, h0:h0 + 4, :]
                link(v.tensor_tensor(s, s, decay[:, h0:h0 + 4, ds(c, 1)].to_broadcast([P, 4, P]), ALU.mult))
                for j in range(4):
                    ins = v.tensor_tensor(state[:, h0 + j, :], ps[UPDATE_BANKS[j]][:, 0:P], state[:, h0 + j, :], ALU.add)
                ins.then_inc(state_ready, 1)

            with dve.Fori(0, 2) as i:
                steps.enter(i, 16)
                for u in range(12):
                    m = U_ATT + u
                    k = 4 * (u // 3) + u % 3
                    ahead(12 * i + m, m)
                    advance(16 * i + k, 8 * i + k // 2, 4 * (k % 2))
                    dve.wait_ge(projected, 12 * i + (m + 1))
                    v.tensor_copy(z_att[:, ds(12 * i + u, 1), :].rearrange("p a t -> p (a t)"), ps[m % 2][:, 0:T])\
                        .then_inc(z_free, 1)
                    if u % 3 == 2:
                        advance(16 * i + k + 1, 8 * i + (k + 1) // 2, 4 * ((k + 1) % 2))
            steps.leave(2)
            advance(32, 16, 0, False)
            advance(33, 16, 4, False, 3)

            dve.wait_ge(bias_ready, 2)
            link(v.memset(stat[:], 1.0))
            v.memset(stat[:, 3:4], 0.0).then_inc(ya_ready, 1)
            for h in range(4):
                dve.wait_ge(o_std, h + 1)
                v.reciprocal(o_rs[:, h, :], o_rs[:, h, :]).then_inc(o_rsqrt, 1)
            dve.wait_ge(o_std, HEADS)
            dve.wait_ge(o_rsqrt, 4)
            rest_rs = o_rs[:].rearrange("p h t -> p (h t)")
            with dve.Fori(0, 2) as i:
                steps.enter(i, 16)
                for u in range(4):
                    m = U_G + u
                    dve.wait_ge(logits, 4 * i + (u + 1))
                    for t in range(2):
                        v.scalar_tensor_tensor(probs[:, t, :], ps[4 + t][:, 0:T], SCALE, bias[:, t, :],
                                               ALU.mult, ALU.add)
                    link(v.scalar_tensor_tensor(probs2[:], ps[4][0:2, T:T + CH], SCALE, bias2[:], ALU.mult, ALU.add))
                    v.tensor_reduce(stat[:, 0:2], probs[:], AX.X, ALU.max)
                    link(v.tensor_reduce(stat[0:2, 2:3], probs2[:], AX.X, ALU.max))
                    v.tensor_scalar(stat[:, 0:3], stat[:, 0:3], -1.0, None, ALU.mult).then_inc(max_ready, 1)
                    piece = rest_rs[:, ds(2 * TQ * i + (4 * TQ + TQ // 2 * u), TQ // 2)]
                    link(v.reciprocal(piece, piece))
                    dve.wait_ge(exp_done, 12 * i + 3 * (u + 1))
                    link(v.reciprocal(stat[:, 8:11], stat[:, 4:7]))
                    for t in range(2):
                        v.tensor_scalar(probs[:, t, :], probs[:, t, :], stat[:, 8 + t:9 + t], None, ALU.mult)
                    v.tensor_scalar(probs2[:], probs2[:], stat[0:2, 10:11], None, ALU.mult).then_inc(p_ready, 1)
                    ahead(4 * i + m, m)
                    h = ds(4 * i + u, 1)
                    rs = o_rs[:, h, :].rearrange("p a t -> p (a t)")
                    o = z_v[:, h, T0:T].rearrange("p a t -> p (a t)")
                    v.scalar_tensor_tensor(o, o, vec_a[:, V_HGN:V_HGN + 1], rs, ALU.mult, ALU.mult)\
                        .then_inc(o_normed, 1)
                    dve.wait_ge(projected, 4 * i + (m + 1))
                    v.tensor_copy(z_g[:, ds(4 * i + u, 1), :].rearrange("p a t -> p (a t)"), ps[m % 2][:, 0:TQ])\
                        .then_inc(z_free, 1)
                    dve.wait_ge(ya_hi_ready, 4 * i + (u + 1))
                    v.tensor_tensor(ya_lo[:, h, :].rearrange("p a t -> p (a t)"), ps[2][:, 0:TQ],
                                    ya_hi[:, h, :].rearrange("p a t -> p (a t)").bitcast(F32), ALU.subtract)\
                        .then_inc(ya_ready, 1)
            steps.leave(2)

            dve.wait_ge(o_normed, HEADS)
            for h in range(HEADS + 1):
                if h < HEADS:
                    o = z_v[:, h, T0:T]
                    dve.wait_ge(g_ready, h + 1)
                    v.tensor_tensor(o, o, z_g[:, h, :], ALU.mult).then_inc(o_gated, 1)
                if h:
                    dve.wait_ge(yh_hi_ready, h)
                    v.tensor_tensor(yh_lo[:, h - 1, :], z_v[:, h - 1, T0:T], yh_hi[:, h - 1, :].bitcast(F32),
                                    ALU.subtract).then_inc(yh_ready, 1)
            ahead(U_MERGE, U_MERGE)

            with dve.Fori(0, 4) as i:
                for u in range(4):
                    m = U_MERGE + u
                    dve.wait_ge(projected, 4 * i + (m + 1))
                    dve.wait_ge(gate_sig, 4 * i + (u + 1))
                    bank = 2 * (u % 2)
                    v.tensor_tensor(gates[u][:, 0, :], ps[bank][:, 0:TQ], gates[u][:, 0, :], ALU.mult)
                    v.tensor_tensor(gates[u][:, 1, :], ps[bank + 1][:, 0:TQ], gates[u][:, 1, :], ALU.mult)\
                        .then_inc(merge_free, 1)
                    dve.wait_ge(merge_free, 4 * i + (u + 3))
                    v.tensor_tensor(gates[u][:, 0, :], gates[u][:, 0, :], gates[u][:, 1, :], ALU.add)\
                        .then_inc(m_sum, 1)
                    ahead(4 * i + (m + 1), m + 1)
                    dve.wait_ge(mh_ready, 4 * i + (u + 1))
                    t = ds(4 * i + u, 1)
                    v.tensor_tensor(m_lo[:, t, :].rearrange("p a t -> p (a t)"), gates[u][:, 0, :],
                                    m_hi[:, t, :].rearrange("p a t -> p (a t)").bitcast(F32), ALU.subtract)\
                        .then_inc(m_ready, 1)

            with dve.Fori(0, 4) as i:
                for u in range(4):
                    m = U_OUT + u
                    dve.wait_ge(projected, 4 * i + (m + 1))
                    dve.wait_ge(xt_ready, 4 * i + (u + 1))
                    h = h_res[:, ds(4 * i + u, 1), :].rearrange("p a t -> p (a t)")
                    v.tensor_tensor(h, ps[u % 2][:, 0:TQ], h, ALU.add).then_inc(out_free, 1)
                    ahead(4 * i + (m + 1), m + 1)

            dve.wait_ge(h_std, 1)
            dve.wait_ge(out_free, 18)
            link(v.reciprocal(h_rs[:], h_rs[:]))

            for k in range(KT + 2):
                if k >= 4 and k < KT:
                    dve.wait_ge(u2l_ready, k - 3)
                if k < KT:
                    v.scalar_tensor_tensor(u_tmp[k % 4][:], h_res[:, k, :], vec_a[:, V_FFN + k:V_FFN + k + 1], h_rs[:],
                                           ALU.mult, ALU.mult).then_inc(u2_ready, 1)
                if k >= 2:
                    dve.wait_ge(u2h_ready, k - 1)
                    v.tensor_tensor(m_lo[:, k - 2, :], u_tmp[(k - 2) % 4][:], m_hi[:, k - 2, :].bitcast(F32),
                                    ALU.subtract).then_inc(u2l_ready, 1)

            for half, (u_ff, u_down) in enumerate(((U_FF, U_DOWN), (U_FF2, U_DOWN2))):
                if half == 1:
                    ahead(u_ff, u_ff)
                with dve.Fori(0, FH // 2) as i:
                    steps.enter(i, 4)

                    def low(a):
                        dve.wait_ge(hidh_ready, 2 * i + (FH * half + a + 1))
                        j = ds(2 * i + a, 1)
                        v.tensor_tensor(hid_lo[:, j, :].rearrange("p a t -> p (a t)"), conv[a][:],
                                        hid_hi[:, j, :].rearrange("p a t -> p (a t)").bitcast(F32), ALU.subtract)\
                            .then_inc(hidl_ready, 1)

                    for u in range(4):
                        m = u_ff + u
                        if u == 3:
                            low(0)
                        dve.wait_ge(projected, 4 * i + (m + 1))
                        if u < 2:
                            tap = lambda vec, c: vec[:, ds(2 * i + (c + FH * half + u), 1)]
                            c = conv[u][:]
                            bank = ps[4 * half + u]
                            link(v.tensor_scalar(c, bank[:, 2:TQ], tap(vec_c, V_C2), tap(vec_a, V_CB),
                                                 ALU.mult, ALU.add))
                            link(v.scalar_tensor_tensor(c, bank[:, 1:TQ - 1], tap(vec_b, V_C1), c, ALU.mult, ALU.add))
                            v.scalar_tensor_tensor(c, bank[:, 0:TQ - 2], tap(vec_b, V_C0), c, ALU.mult, ALU.add)\
                                .then_inc(ff_taken, 1)
                        else:
                            c = conv[u - 2][:]
                            dve.wait_ge(silu_ready, 2 * i + (FH * half + u - 1))
                            v.tensor_tensor(c, ps[4 * half + u][:, 0:SEQ], c, ALU.mult).then_inc(ff_taken, 1)
                        ahead(4 * i + (m + 1), m + 1)
                    low(1)
                steps.leave(FH // 2)

                ahead(u_down + 1, u_down + 1)
                with dve.Fori(0, 4) as i:
                    for u in range(4):
                        ahead(4 * i + (u_down + 2 + u), u_down + 2 + u)
                for n in range(u_down + 18, u_down + FH - 1):
                    ahead(n, n)
                for b in range(8):
                    if b == 4 and half == 1:
                        dve.wait_ge(f_sq_ready, 1)
                        for n in range(1, 4):
                            dve.wait_ge(f_sq_ready, n + 1)
                            link(v.tensor_tensor(f_sq[0][:], f_sq[0][:], f_sq[n][:], ALU.add))
                        v.tensor_tensor(f_sq[0][:, 0, :], f_sq[0][:, 0, :], f_sq[0][:, 1, :], ALU.add)\
                            .then_inc(f_half, 1)
                    if b == 4:
                        ahead(u_down + FH - 1, u_down + FH - 1)
                    if b % 4 == 0:
                        dve.wait_ge(projected, u_down + FH - 1 + b // 4)
                    h = h_res[:].rearrange("p (g u) t -> p u g t", u=2)[:, b // 4, 2 * (b % 4):2 * (b % 4) + 2, 2:TQ]
                    bank = ps[(b + 4 * (half + 1)) % 8]
                    v.tensor_tensor(h, bank[:].rearrange("p (g t) -> p g t", g=2), h, ALU.add).then_inc(down_added, 1)

            dve.wait_ge(f_std, 1)
            v.reciprocal(f_rs[:], f_rs[:]).then_inc(f_rs_ready, 1)
            dve.wait_ge(f_rs_ready, 1)
            for k in range(K_POOL):
                v.scalar_tensor_tensor(h_res[:, k, 2:TQ], h_res[:, k, 2:TQ], vec_c[:, V_FIN + k:V_FIN + k + 1],
                                       f_rs[:], ALU.mult, ALU.mult).then_inc(f_ready, 1)


_INS = ['x', 'meta_tokens', 'attn_norm_w', 'w_in', 'hgrn_lb_logits', 'hgrn_norm_w', 'idx_k_norm_w',
        'w_branch_hgrn', 'w_branch_dsa', 'w_out', 'ffn_norm_w', 'w_ffn_gate', 'w_ffn_up',
        'ffn_conv_w', 'ffn_conv_b', 'w_ffn_down', 'final_norm_w']


def kernel(**inputs):
    import numpy as np
    import concourse.bacc as bacc
    from concourse.bass_utils import run_bass_kernel_spmd as run

    nc = bacc.Bacc("TRN2", target_bir_lowering=False, num_devices=1)
    arrays, args = {}, []
    for name in _INS:
        a = np.ascontiguousarray(inputs[name])
        arrays[f"in_{name}_dram"] = a
        args.append(nc.dram_tensor(f"in_{name}_dram", a.shape, mybir.dt.from_np(a.dtype), kind="ExternalInput").ap())
    args.append(nc.dram_tensor("out_0_dram", (1, SEQ, D), F32, kind="ExternalOutput").ap())
    hybrid_block(nc, *args)
    r = run(nc, [arrays], core_ids=[0])
    return r.results[0]["out_0_dram"]
```
